# Optimizing a Trainium2 kernel written in Bass

```python
import jax, jax.numpy as jnp
from jax import lax
import numpy as np
import math

D_MODEL = 1024
BATCH = 1
SEQ = 512
DEPTH = 1

D_FF = 2816
ROPE_THETA = 10000.0
NORM_EPS = 1e-6
Q_BLOCK = 128
H_A = 8
Q_LORA = 384
KV_LORA = 256
D_NOPE = 64
D_ROPE_A = 32
D_V_A = 64
H_IDX = 8
D_IDX = 32
TOPK_MAX = 256
DIL_PAIRS = ((128, 1), (512, 4), (2048, 16))
N_GROUPS_B = 3
H_B = 4
D_HEAD_B = 64
N_MOD = 9
COLS = (Q_LORA, KV_LORA, D_ROPE_A, D_IDX, H_IDX, 3 * N_GROUPS_B * H_B * D_HEAD_B, 2 * D_MODEL)
D_IN = sum(COLS)
WIDTH_A = H_A * D_V_A
WIDTH_B = H_B * D_HEAD_B


def rms_norm(x, g):
    xf = x.astype(jnp.float32)
    y = xf * lax.rsqrt(jnp.mean(xf * xf, axis=-1, keepdims=True) + NORM_EPS)
    return (y * g.astype(jnp.float32)).astype(x.dtype)

def rope(x, pos):
    d = x.shape[-1]
    half = d // 2
    inv = ROPE_THETA ** (-jnp.arange(half, dtype=jnp.float32) / half)
    ang = pos.astype(jnp.float32)[..., None] * inv
    ang = ang.reshape(ang.shape[:2] + (1,) * (x.ndim - 3) + (half,))
    cos, sin = jnp.cos(ang), jnp.sin(ang)
    xf = x.astype(jnp.float32)
    x1, x2 = xf[..., :half], xf[..., half:]
    return jnp.concatenate([x1 * cos - x2 * sin, x2 * cos + x1 * sin], axis=-1).astype(x.dtype)

def swiglu(h, w_gate, w_up, w_down):
    return (jax.nn.silu(h @ w_gate) * (h @ w_up)) @ w_down

def dsa_branch(c_q, c_kv, k_rope, k_idx, w_idx, pos, w_uq, w_uk, w_uv, w_iq):
    B, S, _ = c_q.shape
    topk = min(TOPK_MAX, S // 4)
    q = jnp.einsum('bsr,rhe->bshe', c_q, w_uq)
    q_nope, q_rope = q[..., :D_NOPE], rope(q[..., D_NOPE:], pos)
    k_rope = rope(k_rope[:, :, None, :], pos)[:, :, 0]
    q_lat = jnp.einsum('bshn,rhn->bshr', q_nope, w_uk)
    q_idx = rope(jnp.einsum('bsr,rhe->bshe', c_q, w_iq), pos)
    k_idx = rope(k_idx[:, :, None, :], pos)[:, :, 0]
    w_idx = w_idx * (H_IDX ** -0.5)
    attn_scale = (D_NOPE + D_ROPE_A) ** -0.5
    idx_scale = D_IDX ** -0.5
    key_pos = jnp.arange(S)
    gather = jax.vmap(lambda a, i: a[i])

    def block(i):
        t0 = i * Q_BLOCK
        tq = t0 + jnp.arange(Q_BLOCK)
        qi = lax.dynamic_slice_in_dim(q_idx, t0, Q_BLOCK, axis=1)
        wi = lax.dynamic_slice_in_dim(w_idx, t0, Q_BLOCK, axis=1)
        logits = jnp.einsum('bqhe,bse->bqhs', qi, k_idx).astype(jnp.float32) * idx_scale
        iscore = jnp.einsum('bqh,bqhs->bqs', wi.astype(jnp.float32), jax.nn.relu(logits))
        causal = key_pos[None, :] <= tq[:, None]
        iscore = jnp.where(causal[None], iscore, -jnp.inf)
        _, sel = lax.top_k(iscore, topk)
        valid = sel <= tq[None, :, None]
        ckv_sel = gather(c_kv, sel)
        kr_sel = gather(k_rope, sel)
        ql = lax.dynamic_slice_in_dim(q_lat, t0, Q_BLOCK, axis=1)
        qr = lax.dynamic_slice_in_dim(q_rope, t0, Q_BLOCK, axis=1)
        s = (jnp.einsum('bqhr,bqkr->bqhk', ql, ckv_sel)
             + jnp.einsum('bqhe,bqke->bqhk', qr, kr_sel)).astype(jnp.float32) * attn_scale
        s = jnp.where(valid[:, :, None, :], s, -jnp.inf)
        p = jax.nn.softmax(s, axis=-1)
        return jnp.einsum('bqhk,bqkr->bqhr', p.astype(c_kv.dtype), ckv_sel)

    o_lat = lax.map(block, jnp.arange(S // Q_BLOCK))
    o_lat = jnp.moveaxis(o_lat, 0, 1).reshape(B, S, H_A, KV_LORA)
    o = jnp.einsum('bshr,rhv->bshv', o_lat, w_uv)
    return o.reshape(B, S, WIDTH_A)

def dilated_group(q, k, v, window, dilation):
    B, S, H, dh = q.shape
    offs = jnp.arange(window // dilation + 1) * dilation
    scale = dh ** -0.5

    def block(i):
        t0 = i * Q_BLOCK
        tq = t0 + jnp.arange(Q_BLOCK)
        idx = tq[:, None] - offs[None, :]
        valid = idx >= 0
        idxc = jnp.maximum(idx, 0)
        kg = k[:, idxc]
        vg = v[:, idxc]
        qb = lax.dynamic_slice_in_dim(q, t0, Q_BLOCK, axis=1)
        s = jnp.einsum('bqhe,bqnhe->bqhn', qb, kg).astype(jnp.float32) * scale
        s = jnp.where(valid[None, :, None, :], s, -jnp.inf)
        lse = jax.nn.logsumexp(s, axis=-1)
        p = jnp.exp(s - lse[..., None])
        o = jnp.einsum('bqhn,bqnhe->bqhe', p.astype(v.dtype), vg)
        return o, lse

    o, lse = lax.map(block, jnp.arange(S // Q_BLOCK))
    o = jnp.moveaxis(o, 0, 1).reshape(B, S, H, dh)
    lse = jnp.moveaxis(lse, 0, 1).reshape(B, S, H)
    return o, lse

def dilated_branch(qkv, pos):
    B, S = qkv.shape[:2]
    q = rope(qkv[:, :, 0], pos)
    k = rope(qkv[:, :, 1], pos)
    v = qkv[:, :, 2]
    outs, lses = [], []
    for g, (window, dilation) in enumerate(DIL_PAIRS):
        o, lse = dilated_group(q[:, :, g], k[:, :, g], v[:, :, g], window, dilation)
        outs.append(o)
        lses.append(lse)
    wts = jax.nn.softmax(jnp.stack(lses, axis=0), axis=0)
    o = jnp.sum(wts[..., None].astype(v.dtype) * jnp.stack(outs, axis=0), axis=0)
    return o.reshape(B, S, WIDTH_B)

def hybrid_mixer(u, pos, w_in, g_cq, g_ckv, w_uq, w_uk, w_uv, w_iq, w_up_a, w_up_b, w_o):
    B, S, _ = u.shape
    proj = u @ w_in
    splits, acc = [], 0
    for n in COLS[:-1]:
        acc += n
        splits.append(acc)
    c_q, c_kv, k_rope, k_idx, w_idx, qkv_b, gates = jnp.split(proj, splits, axis=-1)
    c_q = rms_norm(c_q, g_cq)
    c_kv = rms_norm(c_kv, g_ckv)
    o_a = dsa_branch(c_q, c_kv, k_rope, k_idx, w_idx, pos, w_uq, w_uk, w_uv, w_iq)
    o_b = dilated_branch(qkv_b.reshape(B, S, 3, N_GROUPS_B, H_B, D_HEAD_B), pos)
    g_a, g_b = jnp.split(gates, 2, axis=-1)
    z = jax.nn.sigmoid(g_a) * (o_a @ w_up_a) + jax.nn.sigmoid(g_b) * (o_b @ w_up_b)
    return z @ w_o

def first_inputs(seed: int = 0) -> dict:
    key = jax.random.key(seed)
    ks = jax.random.split(key, 32)
    L, D = DEPTH, D_MODEL

    def nrm(k, shape, fan_in):
        return jax.random.normal(k, shape, jnp.float32) * (fan_in ** -0.5)

    def gain(k, shape):
        return 1.0 + 0.05 * jax.random.normal(k, shape, jnp.float32)

    x = jax.random.normal(ks[0], (BATCH, SEQ, D), jnp.float32)
    c = jax.random.normal(ks[1], (BATCH, D), jnp.float32)
    positions = (jax.random.randint(ks[2], (BATCH, 1), 0, 512, dtype=jnp.int32)
                 + jnp.arange(SEQ, dtype=jnp.int32)[None, :])
    return {
        "x": x,
        "c": c,
        "positions": positions,
        "w_mod": 0.5 * nrm(ks[3], (L, D, N_MOD * D), D),
        "b_mod": 0.01 * jax.random.normal(ks[4], (L, N_MOD * D), jnp.float32),
        "g_pre_ffn1": gain(ks[5], (L, D)),
        "w_gate1": nrm(ks[6], (L, D, D_FF), D),
        "w_up1": nrm(ks[7], (L, D, D_FF), D),
        "w_down1": nrm(ks[8], (L, D_FF, D), D_FF),
        "g_post_ffn1": gain(ks[9], (L, D)),
        "g_pre_mix": gain(ks[10], (L, D)),
        "w_in": nrm(ks[11], (L, D, D_IN), D),
        "g_cq": gain(ks[12], (L, Q_LORA)),
        "g_ckv": gain(ks[13], (L, KV_LORA)),
        "w_uq": nrm(ks[14], (L, Q_LORA, H_A, D_NOPE + D_ROPE_A), Q_LORA),
        "w_uk": nrm(ks[15], (L, KV_LORA, H_A, D_NOPE), KV_LORA),
        "w_uv": nrm(ks[16], (L, KV_LORA, H_A, D_V_A), KV_LORA),
        "w_iq": nrm(ks[17], (L, Q_LORA, H_IDX, D_IDX), Q_LORA),
        "w_up_a": nrm(ks[18], (L, WIDTH_A, D), WIDTH_A),
        "w_up_b": nrm(ks[19], (L, WIDTH_B, D), WIDTH_B),
        "w_o": nrm(ks[20], (L, D, D), D),
        "g_post_mix": gain(ks[21], (L, D)),
        "g_pre_ffn2": gain(ks[22], (L, D)),
        "w_gate2": nrm(ks[23], (L, D, D_FF), D),
        "w_up2": nrm(ks[24], (L, D, D_FF), D),
        "w_down2": nrm(ks[25], (L, D_FF, D), D_FF),
        "g_post_ffn2": gain(ks[26], (L, D)),
    }

def first_block(x, c, positions, w_mod, b_mod, g_pre_ffn1, w_gate1, w_up1, w_down1, g_post_ffn1,
              g_pre_mix, w_in, g_cq, g_ckv, w_uq, w_uk, w_uv, w_iq, w_up_a, w_up_b, w_o, g_post_mix,
              g_pre_ffn2, w_gate2, w_up2, w_down2, g_post_ffn2):
    B = x.shape[0]
    for l in range(DEPTH):
        mod = (jax.nn.silu(c) @ w_mod[l] + b_mod[l]).reshape(B, N_MOD, D_MODEL)
        sh1, sc1, gt1, sh2, sc2, gt2, sh3, sc3, gt3 = [mod[:, j, None, :] for j in range(N_MOD)]
        h = rms_norm(x, g_pre_ffn1[l]) * (1 + sc1) + sh1
        x = x + 0.5 * gt1 * rms_norm(swiglu(h, w_gate1[l], w_up1[l], w_down1[l]), g_post_ffn1[l])
        u = rms_norm(x, g_pre_mix[l]) * (1 + sc2) + sh2
        y = hybrid_mixer(u, positions, w_in[l], g_cq[l], g_ckv[l], w_uq[l], w_uk[l], w_uv[l], w_iq[l],
                         w_up_a[l], w_up_b[l], w_o[l])
        x = x + gt2 * rms_norm(y, g_post_mix[l])
        h = rms_norm(x, g_pre_ffn2[l]) * (1 + sc3) + sh3
        x = x + 0.5 * gt3 * rms_norm(swiglu(h, w_gate2[l], w_up2[l], w_down2[l]), g_post_ffn2[l])
    return x


CHUNK = 64
HG_HEADS = 8
HG_DK = 128
HG_DV = D_MODEL // HG_HEADS
HG_KW = HG_HEADS * HG_DK
HG_VW = HG_HEADS * HG_DV
FOX_HEADS = 8
FOX_DH = 128
FOX_W = FOX_HEADS * FOX_DH
MEM_LEN = 256
MEM_HEADS = 4
MEM_DH = D_MODEL // MEM_HEADS
N_BRANCH = 2
EPS = 1e-6
IN_SPLITS = [HG_KW, HG_KW, HG_VW, HG_VW, FOX_W, FOX_W, FOX_W, FOX_HEADS, N_BRANCH * D_MODEL]
IN_COLS = sum(IN_SPLITS)
IN_OFFSETS = list(np.cumsum(IN_SPLITS)[:-1])


def rmsnorm(x, g):
    x32 = x.astype(jnp.float32)
    y = x32 * lax.rsqrt(jnp.mean(x32 * x32, axis=-1, keepdims=True) + EPS)
    return (y * g.astype(jnp.float32)).astype(x.dtype)

def swiglu_2(h, w_in, w_down):
    gate, up = jnp.split(h @ w_in, 2, axis=-1)
    return (jax.nn.silu(gate) * up) @ w_down

def hgrn2_chunkwise(q, f_logit, inp, lb):
    B, S = q.shape[0], q.shape[1]
    n = S // CHUNK
    f = lb + (1.0 - lb) * jax.nn.sigmoid(f_logit.astype(jnp.float32))
    logf = jnp.log(f)
    k = 1.0 - f
    q = jax.nn.silu(q.astype(jnp.float32))
    inp = inp.astype(jnp.float32)

    def to_chunks(t):
        return t.reshape(B, n, CHUNK, t.shape[2], t.shape[3]).transpose(1, 0, 3, 2, 4)

    qc, kc, ic = to_chunks(q), to_chunks(k), to_chunks(inp)
    bc = jnp.cumsum(to_chunks(logf), axis=3)
    mask = jnp.tril(jnp.ones((CHUNK, CHUNK), dtype=bool))[:, :, None]

    def step(state, xs):
        qt, kt, it, bt = xs
        diff = bt[:, :, :, None, :] - bt[:, :, None, :, :]
        decay = jnp.exp(jnp.where(mask, diff, -jnp.inf))
        a = jnp.einsum('bhtd,bhsd,bhtsd->bhts', qt, kt, decay)
        o_intra = jnp.einsum('bhts,bhsv->bhtv', a, it)
        o_inter = jnp.einsum('bhtd,bhdv->bhtv', qt * jnp.exp(bt), state)
        b_last = bt[:, :, -1:, :]
        new_state = jnp.exp(b_last[:, :, 0, :])[..., None] * state + jnp.einsum(
            'bhsd,bhsv->bhdv', kt * jnp.exp(b_last - bt), it)
        return new_state, o_intra + o_inter

    s0 = jnp.zeros((B, q.shape[2], HG_DK, HG_DV), jnp.float32)
    _, o = lax.scan(step, s0, (qc, kc, ic, bc))
    return o.transpose(1, 0, 3, 2, 4).reshape(B, S, HG_VW)

def fox_attention(q, k, v, f_logit):
    B, S, H, dh = q.shape
    n_blk = S // Q_BLOCK
    scale = 1.0 / math.sqrt(dh)
    c = jnp.cumsum(jax.nn.log_sigmoid(f_logit.astype(jnp.float32)), axis=1).transpose(0, 2, 1)
    k32 = k.astype(jnp.float32)
    v32 = v.astype(jnp.float32)
    qb = q.astype(jnp.float32).reshape(B, n_blk, Q_BLOCK, H, dh).transpose(1, 0, 3, 2, 4)
    cb = c.reshape(B, H, n_blk, Q_BLOCK).transpose(2, 0, 1, 3)
    kpos = jnp.arange(S)

    def block(args):
        qi, ci, blk = args
        s = jnp.einsum('bhqd,bkhd->bhqk', qi, k32) * scale
        s = s + ci[..., None] - c[:, :, None, :]
        qpos = blk * Q_BLOCK + jnp.arange(Q_BLOCK)
        s = jnp.where(kpos[None, :] <= qpos[:, None], s, -jnp.inf)
        p = jax.nn.softmax(s, axis=-1)
        return jnp.einsum('bhqk,bkhd->bqhd', p, v32)

    o = lax.map(block, (qb, cb, jnp.arange(n_blk)))
    return o.transpose(1, 0, 2, 3, 4).reshape(B, S, H * dh)

def mem_cross_attention(h, mem_n, w_mq, w_mkv, w_mo):
    B, S, _ = h.shape
    q = (h @ w_mq).reshape(B, S, MEM_HEADS, MEM_DH).astype(jnp.float32)
    k, v = jnp.split(mem_n @ w_mkv, 2, axis=-1)
    k = k.reshape(B, MEM_LEN, MEM_HEADS, MEM_DH).astype(jnp.float32)
    v = v.reshape(B, MEM_LEN, MEM_HEADS, MEM_DH).astype(jnp.float32)
    s = jnp.einsum('bqhd,bkhd->bhqk', q, k) * (1.0 / math.sqrt(MEM_DH))
    p = jax.nn.softmax(s, axis=-1)
    o = jnp.einsum('bhqk,bkhd->bqhd', p, v).reshape(B, S, D_MODEL).astype(h.dtype)
    return o @ w_mo

def second_inputs(seed: int = 0) -> dict:
    key = jax.random.key(seed)
    ks = iter(jax.random.split(key, 40))
    f32 = jnp.float32

    def w(shape, fan_in):
        return jax.random.normal(next(ks), shape, f32) * (fan_in ** -0.5)

    def gain(shape):
        return 1.0 + 0.05 * jax.random.normal(next(ks), shape, f32)

    L, D = DEPTH, D_MODEL
    return {
        "x": jax.random.normal(next(ks), (BATCH, SEQ, D), f32),
        "mem": jax.random.normal(next(ks), (BATCH, MEM_LEN, D), f32),
        "ffn1_pre_g": gain((L, D)),
        "ffn1_w_in": w((L, D, 2 * D_FF), D),
        "ffn1_w_down": w((L, D_FF, D), D_FF),
        "ffn1_post_g": gain((L, D)),
        "mix_pre_g": gain((L, D)),
        "w_in": w((L, D, IN_COLS), D),
        "hg_lb_logits": 0.5 * jax.random.normal(next(ks), (L + 1, HG_HEADS, HG_DK), f32),
        "hg_norm_g": gain((L, HG_VW)),
        "fox_f_bias": 1.0 + 0.5 * jax.random.normal(next(ks), (L, FOX_HEADS), f32),
        "w_branch_a": w((L, HG_VW, D), HG_VW),
        "w_branch_b": w((L, FOX_W, D), FOX_W),
        "b_gate": 0.02 * jax.random.normal(next(ks), (L, N_BRANCH * D), f32),
        "w_out": w((L, D, D), D),
        "mix_post_g": gain((L, D)),
        "mem_pre_g": gain((L, D)),
        "mem_kv_g": gain((L, D)),
        "w_mq": w((L, D, D), D),
        "w_mkv": w((L, D, 2 * D), D),
        "w_mo": w((L, D, D), D),
        "mem_post_g": gain((L, D)),
        "ffn2_pre_g": gain((L, D)),
        "ffn2_w_in": w((L, D, 2 * D_FF), D),
        "ffn2_w_down": w((L, D_FF, D), D_FF),
        "ffn2_post_g": gain((L, D)),
    }

def second_block(x, mem, ffn1_pre_g, ffn1_w_in, ffn1_w_down, ffn1_post_g,
              mix_pre_g, w_in, hg_lb_logits, hg_norm_g, fox_f_bias,
              w_branch_a, w_branch_b, b_gate, w_out, mix_post_g,
              mem_pre_g, mem_kv_g, w_mq, w_mkv, w_mo, mem_post_g,
              ffn2_pre_g, ffn2_w_in, ffn2_w_down, ffn2_post_g):
    B, S, D = x.shape
    lb_all = jnp.cumsum(jax.nn.softmax(hg_lb_logits.astype(jnp.float32), axis=0), axis=0)
    for l in range(DEPTH):
        h = rmsnorm(x, ffn1_pre_g[l])
        x = x + 0.5 * rmsnorm(swiglu_2(h, ffn1_w_in[l], ffn1_w_down[l]), ffn1_post_g[l])

        h = rmsnorm(x, mix_pre_g[l])
        q_a, f_a, i_a, g_a, q_b, k_b, v_b, f_b, gates = jnp.split(h @ w_in[l], IN_OFFSETS, axis=-1)

        o_a = hgrn2_chunkwise(q_a.reshape(B, S, HG_HEADS, HG_DK),
                              f_a.reshape(B, S, HG_HEADS, HG_DK),
                              i_a.reshape(B, S, HG_HEADS, HG_DV), lb_all[l])
        o_a = rmsnorm(o_a.astype(x.dtype), hg_norm_g[l]) * jax.nn.silu(g_a)
        y_a = o_a @ w_branch_a[l]

        o_b = fox_attention(q_b.reshape(B, S, FOX_HEADS, FOX_DH),
                            k_b.reshape(B, S, FOX_HEADS, FOX_DH),
                            v_b.reshape(B, S, FOX_HEADS, FOX_DH),
                            f_b + fox_f_bias[l])
        y_b = o_b.astype(x.dtype) @ w_branch_b[l]

        gate = jax.nn.sigmoid((gates + b_gate[l]).astype(jnp.float32)).reshape(B, S, N_BRANCH, D)
        y = (gate[:, :, 0] * y_a.astype(jnp.float32) + gate[:, :, 1] * y_b.astype(jnp.float32)).astype(x.dtype)
        x = x + rmsnorm(y @ w_out[l], mix_post_g[l])

        h = rmsnorm(x, mem_pre_g[l])
        mem_n = rmsnorm(mem, mem_kv_g[l])
        x = x + rmsnorm(mem_cross_attention(h, mem_n, w_mq[l], w_mkv[l], w_mo[l]), mem_post_g[l])

        h = rmsnorm(x, ffn2_pre_g[l])
        x = x + 0.5 * rmsnorm(swiglu_2(h, ffn2_w_in[l], ffn2_w_down[l]), ffn2_post_g[l])
    return x


def setup_inputs(seed=0):
    out = dict(first_inputs(seed))
    for name, value in second_inputs(seed + 1).items():
        if name != "x":
            out[name + "_2"] = value
    return out


def reference(
    x, c, positions, w_mod, b_mod, g_pre_ffn1, w_gate1, w_up1, w_down1, g_post_ffn1, g_pre_mix,
    w_in, g_cq, g_ckv, w_uq, w_uk, w_uv, w_iq, w_up_a, w_up_b, w_o, g_post_mix, g_pre_ffn2,
    w_gate2, w_up2, w_down2, g_post_ffn2, mem_2, ffn1_pre_g_2, ffn1_w_in_2, ffn1_w_down_2,
    ffn1_post_g_2, mix_pre_g_2, w_in_2, hg_lb_logits_2, hg_norm_g_2, fox_f_bias_2, w_branch_a_2,
    w_branch_b_2, b_gate_2, w_out_2, mix_post_g_2, mem_pre_g_2, mem_kv_g_2, w_mq_2, w_mkv_2,
    w_mo_2, mem_post_g_2, ffn2_pre_g_2, ffn2_w_in_2, ffn2_w_down_2, ffn2_post_g_2,
):
    x = first_block(
        x, c, positions, w_mod, b_mod, g_pre_ffn1, w_gate1, w_up1, w_down1, g_post_ffn1,
        g_pre_mix, w_in, g_cq, g_ckv, w_uq, w_uk, w_uv, w_iq, w_up_a, w_up_b, w_o, g_post_mix,
        g_pre_ffn2, w_gate2, w_up2, w_down2, g_post_ffn2,
    )
    return second_block(
        x, mem_2, ffn1_pre_g_2, ffn1_w_in_2, ffn1_w_down_2, ffn1_post_g_2, mix_pre_g_2, w_in_2,
        hg_lb_logits_2, hg_norm_g_2, fox_f_bias_2, w_branch_a_2, w_branch_b_2, b_gate_2,
        w_out_2, mix_post_g_2, mem_pre_g_2, mem_kv_g_2, w_mq_2, w_mkv_2, w_mo_2, mem_post_g_2,
        ffn2_pre_g_2, ffn2_w_in_2, ffn2_w_down_2, ffn2_post_g_2,
    )


_drawn_inputs = setup_inputs


def setup_inputs(seed=0):
    import zlib

    import numpy as np

    out = dict(_drawn_inputs(seed))
    spreads = {}
    factors = {'g_pre_ffn1': 2.804,
     'g_post_ffn1': 3.782,
     'g_pre_ffn2': 4.129,
     'g_post_ffn2': 5.679,
     'b_gate_2': 8.0,
     'ffn2_pre_g_2': 3.133,
     'ffn2_post_g_2': 4.302}
    for name, (base, spread) in spreads.items():
        noise = np.random.default_rng([zlib.crc32(name.encode()), seed]).standard_normal(out[name].shape)
        drawn = base * np.exp(spread * noise) if base else spread * noise
        out[name] = __import__('jax').numpy.asarray(drawn.astype(out[name].dtype))
    for name, factor in factors.items():
        out[name] = (out[name] * factor).astype(out[name].dtype)
    return out
```

```python
import math
from contextlib import contextmanager

import concourse.bass as bass
import numpy as np
from concourse import mybir

F32 = mybir.dt.float32
F32R = mybir.dt.float32r
I32 = mybir.dt.int32
U8 = mybir.dt.uint8
ALU = mybir.AluOpType
ACT = mybir.ActivationFunctionType
ENG = mybir.EngineType

P = 128
S = 512
D = 1024
FF = 2816
DB = D // P
FB = FF // P
TT = S // P
CH = 2048
NMOD = 9 * DB
MBLK = 5
M_FIRST = NMOD - (FB // 2) * MBLK
EPS = 1e-6
NEG = -1e30

NOPE, ROPE_A, D_QK, Q_LORA, KV_LORA, TOPK = 64, 32, 96, 384, 256, 128
H_A, H_IDX, H_B, HG, FOX, MEM_H, MEM = 8, 8, 4, 8, 8, 4, 256


class Ticket:

    def __init__(self, track, value, k=0, loop=None):
        self.track, self.value, self.k, self.loop = track, value, k, loop

    def last(self, back=0):
        if self.loop is None or not self.loop.closed:
            return self
        start, stride = self.loop.start[self.track], self.loop.stride[self.track]
        return Ticket(self.track, start + (self.loop.n - 1 - back) * stride + self.k)


class Track:

    def __init__(self, nc, name, eng=None, head_start=0):
        self.name, self.eng, self.sem = name, eng, nc.alloc_semaphore("s_" + name)
        self.base, self.k, self.stride, self.loop = 0, 0, 0, None
        if head_start:
            eng.sem_inc(self.sem, head_start)
            self.base = head_start

    def mark(self, ins, by=1):
        ins.then_inc(self.sem, by)
        self.k += by
        return self.now()

    def now(self):
        return Ticket(self, self.base + self.k, self.k, self.loop)


class Loop:

    def __init__(self, n):
        self.n, self.start, self.stride, self.closed = n, {}, {}, False


class Counting:

    def __init__(self, nc, before):
        self.nc, self.before, self.counted = nc, before, {}
        self.tracks, self.steps, self.inside, self.seen, self.number = {}, {}, None, {}, 0

    def track(self, name, eng=None, head_start=0):
        self.tracks[name] = Track(self.nc, name, eng, head_start)
        return self.tracks[name]

    def next_name(self):
        self.number += 1
        return self.number

    def wait(self, eng, *tickets):
        for t in tickets:
            if t is None:
                continue
            t = t.last()
            if isinstance(t.value, int):
                key = (str(eng.engine), t.track.name)
                if t.value <= self.seen.get(key, 0):
                    continue
                self.seen[key] = t.value
            eng.wait_ge(t.track.sem, t.value)

    def step(self, name, ticket):
        self.steps[name] = ticket

    def latest(self, name):
        t, lp = self.steps.get(name), self.inside
        if lp is not None and (t is None or t.loop is not lp[0]) and name in lp[1]:
            track, k = lp[1][name]
            track = self.tracks[track]
            return Ticket(track, track.base + (k - track.stride))
        return t

    def meet(self):
        tickets = [Ticket(t, t.base + t.k) for t in self.tracks.values() if t.eng is not None]
        for ticket in tickets:
            self.wait(ticket.track.eng, *tickets)

    @contextmanager
    def loop(self, n):
        key = len(self.counted)
        self.counted[key] = None
        known = self.before.get(key, {"stride": {}, "steps": {}})
        lp, seen = Loop(n), dict(self.seen)
        with self.nc.Fori(0, n, engines=[ENG.PE, ENG.Activation, ENG.DVE]) as i:
            for name, t in self.tracks.items():
                lp.start[t] = t.base + t.k
                lp.stride[t] = t.stride = known["stride"].get(name, 0)
                t.base = i * t.stride + lp.start[t] if t.stride else lp.start[t]
                t.k, t.loop = 0, lp
            self.inside = (lp, known["steps"])
            yield i
        self.inside = None
        self.counted[key] = {"stride": {name: t.k for name, t in self.tracks.items()},
                             "steps": {name: (t.track.name, t.k) for name, t in self.steps.items() if t.loop is lp}}
        assert key not in self.before or known == self.counted[key], "the two builds differ"
        for t in self.tracks.values():
            lp.stride[t] = t.k
            t.base, t.k, t.stride, t.loop = lp.start[t] + n * t.k, 0, 0, None
        lp.closed = True
        self.seen = seen




VECS = [("c", DB), ("b_mod", NMOD), ("g_pre_ffn1", DB), ("g_post_ffn1", DB), ("g_pre_mix", DB),
        ("g_cq", Q_LORA // P), ("g_ckv", KV_LORA // P), ("g_post_mix", DB), ("g_pre_ffn2", DB),
        ("g_post_ffn2", DB), ("ffn1_pre_g_2", DB), ("ffn1_post_g_2", DB), ("mix_pre_g_2", DB),
        ("hg_norm_g_2", DB), ("b_gate_2", 2 * DB), ("mix_post_g_2", DB), ("mem_pre_g_2", DB),
        ("mem_kv_g_2", DB), ("mem_post_g_2", DB), ("ffn2_pre_g_2", DB), ("ffn2_post_g_2", DB),
        ("hg_lb_logits_2", 2 * DB)]
VEC_AT = {name: sum(n for _, n in VECS[:i]) for i, (name, _) in enumerate(VECS)}
NVEC = sum(n for _, n in VECS)


def constants():
    i = np.arange(P)
    q, k = i[:, None], i[None, :]
    c = {"ident": (q == k) * 1.0, "causal": np.where(k <= q, 0.0, NEG)}
    for m in range(7):
        d = 4 * (q - k) - (m - 3)
        c[f"near{m}"] = np.where((d >= 0) & (d <= 128), 0.0, NEG)
    c["far1"] = c["causal"]
    c["far2"] = np.where((q >= k) & ((q - k) % 4 == 0), 0.0, NEG)

    def rotation(half, start=0, stop=P):
        r = np.zeros((P, P))
        for p in range(start, stop):
            first = p % (2 * half) < half
            r[p, p + half if first else p - half] = -1.0 if first else 1.0
        return r

    pick_ki, pick_kr = np.zeros((P, P)), np.zeros((P, P))
    pick_ki[i, 32 + i % 32] = 1.0
    pick_kr[NOPE + i[:ROPE_A], i[:ROPE_A]] = 1.0
    rot_q = rotation(16, NOPE, D_QK)
    for name, m in (("rot32", rotation(16)), ("rot64", rotation(32)), ("rot_q", rot_q),
                    ("pick_ki", pick_ki), ("rot_ki", rotation(16) @ pick_ki),
                    ("pick_kr", pick_kr), ("rot_kr", rot_q @ pick_kr)):
        c[name] = m.T
    f32 = np.float32
    inv16 = f32(10000.0) ** (-np.arange(16, dtype=f32) / f32(16))
    inv32 = f32(10000.0) ** (-np.arange(32, dtype=f32) / f32(32))
    c["inv"] = np.stack([inv16[i % 16], inv32[i % 32]], 1)
    c["reset"] = np.ones((P, 1)) * (np.arange(S) % P != 0)
    lev = np.zeros((P, 8, P))
    lev[:, 0] = q == k
    for j in range(7):
        w = 2 << j
        lev[:, j + 1] = (q // w == k // w) & (q % w < w // 2) & (k % w >= w // 2)
    c["levels"] = lev.reshape(P, 8 * P)
    at, n = {}, 0
    for name, a in c.items():
        at[name] = n
        n += a.shape[1]
    return np.concatenate([a.astype(f32) for a in c.values()], 1), at


CONSTS, CONST_AT = constants()


def build(nc, io, counts, upto):
    g = Counting(nc, counts)
    wait, step, latest, meet = g.wait, g.step, g.latest, g.meet
    pe, act, dve, pool, sp = nc.tensor, nc.scalar, nc.vector, nc.gpsimd, nc.sync
    PE, AC, DV = (g.track(n, e, 512) for n, e in (("pe", pe), ("act", act), ("dve", dve)))

    def do(track, waits, fn, *args, **kw):
        wait(track.eng, *waits)
        return track.mark(fn(*args, **kw))

    def sb(name, shape, dt, kb):
        return nc.alloc_sbuf_tensor_at(name, shape, dt, offset=512 + int(round(kb * 1024)))

    X = sb("X", [P, DB, S], F32, 0)
    RAW = sb("RAW", [P, 2, CH], F32, 16)
    WHI = sb("WHI", [P, 2, CH], F32R, 32)
    WLO = sb("WLO", [P, 2, CH], F32R, 48)
    AHI = sb("AHI", [P, DB, S], F32R, 64)
    ALO = sb("ALO", [P, DB, S], F32R, 80)
    ONES = sb("ONES", [P, P], F32, 96)
    IDENT = sb("IDENT", [P, P], F32, 96.5)
    CAUSAL = sb("CAUSAL", [P, P], F32, 97)
    VEC = sb("VEC", [P, NVEC], F32, 97.5)
    MOD = sb("MOD", [P, NMOD], F32, 98.75)
    COEF = sb("COEF", [P, 16 * DB], F32, 99.125)
    CCOL = sb("CCOL", [P, DB], F32, 99.6875)
    EPSC = sb("EPSC", [P, 1], F32, 99.75)
    RIN = sb("RIN", [P, S], F32, 100)
    SSQ = sb("SSQ", [P, S], F32, 102)
    R = 104
    PS = nc.alloc_psum_tensor("PS", [P, 8, S], F32)

    def vec(name, d=0, n=DB):
        return VEC[:, VEC_AT[name] + d:VEC_AT[name] + d + n]

    n_chunks = io["weights"].shape[0]
    loaded = [nc.alloc_semaphore("s_loaded0"), nc.alloc_semaphore("s_loaded1")]
    s_high, s_low = nc.alloc_semaphore("s_high"), nc.alloc_semaphore("s_low")
    stream = {"fed": 0, "taken": 0, "free": [], "per": 0, "i": None}

    def start_stream():
        for j in range(2):
            sp.dma_start(RAW[:, j], io["weights"][j]).then_inc(loaded[j], 16)
        with sp.Fori(1, n_chunks // 2) as i:
            for j in range(2):
                sp.wait_ge(s_low, i * 2 + (j - 1))
                sp.dma_start(RAW[:, j], io["weights"][bass.ds(i * 2 + j, 1)].rearrange("a p c -> (a p) c")) \
                    .then_inc(loaded[j], 16)
        with pool.Fori(0, n_chunks // 2) as i:
            for j in range(2):
                pool.wait_ge(s_high, i * 2 + (j + 1))
                pool.tensor_tensor(WLO[:, j], RAW[:, j], WHI[:, j].bitcast(F32), ALU.subtract) \
                    .then_inc(s_low, 1)

    def feed():
        if stream["i"] is None and stream["fed"] == n_chunks:
            return
        slot, turn = stream["fed"] % 2, stream["fed"] // 2 + 1
        if stream["i"] is not None:
            turn = stream["i"] * (stream["per"] // 2) + turn
        if stream["free"]:
            wait(act, stream["free"].pop(0))
        act.wait_ge(loaded[slot], turn * 16)
        act.activation(WHI[:, slot], RAW[:, slot], ACT.Copy).then_inc(s_high, 1)
        stream["fed"] += 1

    def take():
        n = stream["taken"] + 1
        if stream["i"] is not None:
            n = stream["i"] * stream["per"] + n
        pe.wait_ge(s_low, n)
        stream["taken"] += 1
        return (stream["taken"] - 1) % 2

    def used(ticket):
        stream["free"].append(ticket)

    @contextmanager
    def wloop(n, per):
        with g.loop(n) as i:
            stream["i"], stream["per"] = i, per
            fed, taken = stream["fed"], stream["taken"]
            yield i
            assert stream["fed"] == fed + per and stream["taken"] == taken + per and per % 2 == 0
            stream["i"], stream["per"] = None, 0
        stream["fed"], stream["taken"] = fed + n * per, taken + n * per

    def products(out, slot, pairs, first=True, last=True, weights_move=False):
        n, m = len(pairs), None
        for q, (cols, (hi, lo)) in enumerate(pairs):
            for r, (wt, x) in enumerate(((WHI, hi), (WHI, lo), (WLO, hi))):
                a, b = (x, wt[:, slot, cols]) if weights_move else (wt[:, slot, cols], x)
                m = pe.matmul(out, a, b, start=first and q == 0 and r == 0,
                              stop=last and q == n - 1 and r == 2)
        return m

    def linear(bank, slot, at, step, rhs, width=P, rows=P):
        wait(pe, latest(f"bank {bank} read"))
        n = rhs[0][0].shape[-1]
        m = products(PS[0:rows, bank, 0:n], slot,
                     [(slice(at + q * step, at + q * step + width), x) for q, x in enumerate(rhs)])
        return PE.mark(m)

    A = [(AHI[:, k], ALO[:, k]) for k in range(DB)]

    def split_from(src, hi, lo, waits, bias=None):
        if bias is None:
            t1 = do(AC, waits, act.activation, hi, src, ACT.Copy)
            t2 = do(DV, [t1], dve.tensor_tensor, lo, src, hi.bitcast(F32), ALU.subtract)
        else:
            t1 = do(AC, waits, act.activation, hi, src, ACT.Identity, bias=bias)
            t2 = do(DV, [t1], dve.scalar_tensor_tensor, out=lo, in0=src, scalar=bias,
                    in1=hi.bitcast(F32), op0=ALU.add, op1=ALU.subtract)
        return t2

    def root_mean(bank, sums_t, n, out, rows=P):
        t = do(AC, [sums_t], act.activation, out, PS[:, bank, 0:out.shape[-1]], ACT.Ln, bias=EPSC[:, 0:1],
               scale=1.0 / n)
        step(f"bank {bank} read", t)
        return do(AC, [t], act.activation, out, out, ACT.Exp, scale=-0.5)

    def prenorm(x_t, mul, shift=None):
        SQ = sb(f"SQ{g.next_name()}", [P, 2, S], F32, R + 88)
        T = sb(f"T{g.next_name()}", [P, 3, S], F32, R + 92)
        sq_t, mm_t = [], []
        wait(act, x_t[0])
        wait(dve, x_t[-1])
        wait(pe, latest("bank 0 read"))
        for d in range(DB):
            sq_t.append(do(AC, [x_t[d], mm_t[d - 2] if d > 1 else None], act.activation,
                           SQ[:, d % 2], X[:, d], ACT.Square))
            mm_t.append(do(PE, [sq_t[d]], pe.matmul, PS[:, 0], ONES[:, :], SQ[:, d % 2],
                           start=d == 0, stop=d == DB - 1))
        r = root_mean(0, mm_t[-1], D, RIN[:, :])
        wait(act, *mm_t[-1:])
        a_t, high_t = [], []
        for d in range(DB + 1):
            if d < DB:
                t = do(DV, [r, a_t[d - 3] if d > 2 else None], dve.scalar_tensor_tensor, out=T[:, d % 3], in0=X[:, d],
                       scalar=mul[:, d:d + 1], in1=RIN[:, :], op0=ALU.mult, op1=ALU.mult)
                high_t.append(do(AC, [t], act.activation, AHI[:, d], T[:, d % 3], ACT.Identity,
                                 bias=0.0 if shift is None else shift[:, d:d + 1]))
            if d > 0:
                e = d - 1
                a_t.append(do(DV, [high_t[e]], dve.scalar_tensor_tensor, out=ALO[:, e], in0=T[:, e % 3],
                              scalar=0.0 if shift is None else shift[:, e:e + 1],
                              in1=AHI[:, e].bitcast(F32), op0=ALU.add, op1=ALU.subtract))
        return a_t

    def sum_of_blocks(bank, waits):
        wait(pe, latest(f"bank {bank} read"))
        return do(PE, waits, pe.matmul, PS[:, bank], ONES[:, :], SSQ[:, :], start=True, stop=True)

    def residual(Y, y_t, ssq_t, bank, coef):
        T = sb(f"T{g.next_name()}", [P, 3, S], F32, R + 92)
        r = root_mean(bank, sum_of_blocks(bank, [ssq_t]), D, RIN[:, :])
        x_t, t = [], [None] * DB
        for d in range(DB + 1):
            if d < DB:
                t[d] = do(DV, [r, y_t[d], x_t[d - 3] if d > 2 else None], dve.scalar_tensor_tensor,
                          out=T[:, d % 3], in0=Y[:, d],
                          scalar=coef[:, d:d + 1], in1=RIN[:, :], op0=ALU.mult, op1=ALU.mult)
            if d > 0:
                x_t.append(do(DV, [t[d - 1]], dve.tensor_tensor, X[:, d - 1], X[:, d - 1],
                              T[:, (d - 1) % 3], ALU.add))
        return x_t

    def take_output(Y, SQ, bank, d, mm_t, ssq):
        wait(act, latest(f"sq{d % 2} used"))
        y = do(DV, [mm_t], dve.tensor_copy, Y[:, d], PS[:, bank])
        s = do(AC, [y], act.activation, SQ[:, d % 2], Y[:, d], ACT.Square)
        step(f"bank {bank} read", y)
        if ssq is None:
            ssq = do(DV, [s], dve.tensor_copy, SSQ[:, :], SQ[:, d % 2])
        else:
            ssq = do(DV, [s, ssq], dve.tensor_tensor, SSQ[:, :], SSQ[:, :], SQ[:, d % 2], ALU.add)
        step(f"sq{d % 2} used", ssq)
        return y, ssq

    def ffn(a_t, coef, between=None, late=None):
        u = g.next_name()
        HHI = sb(f"HHI{u}", [P, FB, S], F32R, R)
        HLO = sb(f"HLO{u}", [P, FB, S], F32R, R + 44)
        SIL = sb(f"SIL{u}", [P, 2, S], F32, R + 88)
        PRD = sb(f"PRD{u}", [P, 2, S], F32, R + 92)
        Y = sb(f"Y{u}", [P, DB, S], F32, R + 98)
        meet()
        with wloop(FB // 2, 2) as i:
            if between:
                between[0](i)
            slot = take()
            gate_t = [linear(f, slot, f * P, 2 * P, A) for f in range(2)]
            used(gate_t[1])
            sil_t = []
            for f in range(2):
                wait(act, latest(f"sil{f} used"))
                sil_t.append(do(AC, [gate_t[f]], act.activation, SIL[:, f], PS[:, f], ACT.Silu))
                step(f"bank {f} read", sil_t[f])
            feed()
            if between:
                between[1](i)
                between[2](i)
            slot = take()
            up_t = [linear(2 + f, slot, f * P, 2 * P, A) for f in range(2)]
            used(up_t[1])
            prd_t, hi_t = [], []
            for f in range(2):
                wait(dve, latest(f"prd{f} used"))
                prd_t.append(do(DV, [up_t[f], sil_t[f]], dve.tensor_tensor, PRD[:, f], PS[:, 2 + f],
                                SIL[:, f], ALU.mult))
                step(f"bank {2 + f} read", prd_t[f])
                step(f"sil{f} used", prd_t[f])
                hi_t.append(do(AC, [prd_t[f]], act.activation, HHI[:, bass.ds(i * 2 + f, 1)],
                               PRD[:, f:f + 1], ACT.Copy))
            for f in range(2):
                h_t = do(DV, [hi_t[f]], dve.tensor_tensor, HLO[:, bass.ds(i * 2 + f, 1)], PRD[:, f:f + 1],
                         HHI[:, bass.ds(i * 2 + f, 1)].bitcast(F32), ALU.subtract)
                step(f"prd{f} used", h_t)
            feed()
        order = [4, 5, 6, 7, 0, 1, 2, 3]

        def down(blocks, first=False, last=False):
            slot = take()
            for d in order:
                if first:
                    wait(pe, latest(f"bank {d} read"))
                m = products(PS[:, d], slot, [(slice(k * D + d * P, k * D + (d + 1) * P), x)
                                              for k, x in enumerate(blocks)], first=first, last=last)
                if last:
                    y_mm[d] = PE.mark(m)
            if last:
                return slot
            used(PE.mark(m))
            feed()

        y_mm = {}
        wait(pe, h_t.last(back=1))
        down([(HHI[:, k], HLO[:, k]) for k in range(2)], first=True)
        wait(pe, h_t)
        with wloop(FB // 4 - 1, 2) as i:
            for j in range(2):
                down([(HHI[:, bass.ds(i * 4 + (2 * j + 2 + k), 1)].rearrange("p a s -> p (a s)"),
                       HLO[:, bass.ds(i * 4 + (2 * j + 2 + k), 1)].rearrange("p a s -> p (a s)"))
                      for k in range(2)])
        down([(HHI[:, k], HLO[:, k]) for k in (FB - 4, FB - 3)])
        down([(HHI[:, k], HLO[:, k]) for k in (FB - 2, FB - 1)], last=True)
        y_t, ssq = {}, None
        wait(dve, h_t)
        if late:
            late()
        if between:
            dve.wait_ge(s_mw[1].sem, first_mw + 16 * (FB // 2))
        for d in order:
            y_t[d], ssq = take_output(Y, SIL, d, d, y_mm[d], ssq)
        used(y_mm[order[-1]])
        feed()
        return residual(Y, y_t, ssq, order[0], coef)

    s_in, s_x, s_id = g.track("in"), g.track("x"), g.track("id")
    t_vec = s_in.mark(sp.dma_start(VEC[:, :], io["vecs"]), by=16)
    MW = [sb("MW0", [P, MBLK, D], F32, R), sb("MW1", [P, MBLK, D], F32, R + 99)]
    s_mw = [g.track("mw0"), g.track("mw1")]
    groups = [(b, min(MBLK, M_FIRST - b)) for b in range(0, M_FIRST, MBLK)]
    which = [(len(groups) - 1 - n) % 2 for n in range(len(groups))]
    mw_t = []
    eps_t = do(DV, [], dve.memset, EPSC[:, :], EPS)
    ones_t = do(DV, [], dve.memset, ONES[:, :], 1.0)
    wait(pe, ones_t)
    silu_c = do(AC, [t_vec], act.activation, CCOL[:, :], vec("c"), ACT.Silu)

    def weigh_rows(waits, which, nb):
        wait(dve, silu_c, *waits)
        part = [MW[which][:, 0:nb, k * P:(k + 1) * P] for k in range(DB)]
        t = [None, None]
        for k in range(DB):
            if k < 2:
                t[k] = do(DV, [], dve.tensor_scalar, part[k], part[k], CCOL[:, k:k + 1], None, ALU.mult)
            else:
                t[k % 2] = do(DV, [t[k % 2]], dve.scalar_tensor_tensor, out=part[k % 2], in0=part[k],
                              scalar=CCOL[:, k:k + 1], in1=part[k % 2], op0=ALU.mult, op1=ALU.add)
        return t

    def mod_columns(t, which, b0, nb):
        wait(pe, latest("bank 4 read"))
        wait(pe, *t)
        for b in range(nb):
            for k in range(2):
                m = pe.matmul(PS[:, 4, b:b + 1], MW[which][:, b, k * P:(k + 1) * P], ONES[:, 0:1],
                              start=k == 0, stop=k == 1)
        mm = PE.mark(m)
        off = VEC_AT["b_mod"]
        at, vat = (slice(b0, b0 + nb), slice(off + b0, off + b0 + nb)) if isinstance(b0, int) \
            else (bass.ds(b0, nb), bass.ds(b0 + off, nb))
        t = do(DV, [mm, t_vec], dve.tensor_tensor, MOD[:, at], PS[:, 4, 0:nb], VEC[:, vat], ALU.add)
        step("bank 4 read", t)
        step(f"mw{which} used", mm)
        return t

    for n, (b0, nb) in enumerate(groups):
        if n == 2:
            x_in = s_x.mark(sp.dma_start(X[:, :, :], io["xT"].rearrange("(k p) n -> p k n", p=P)), by=16)
            t_id = s_id.mark(sp.dma_start(IDENT[:, :], io["consts"][:, CONST_AT["ident"]:CONST_AT["ident"] + P]), by=16)
            t_id = s_id.mark(sp.dma_start(CAUSAL[:, :], io["consts"][:, CONST_AT["causal"]:CONST_AT["causal"] + P]), by=16)
        if n >= 2:
            wait(sp, latest(f"mw{which[n]} used"))
        mw_t.append(s_mw[which[n]].mark(sp.dma_start(MW[which[n]][:, 0:nb], io["w_mod"][:, b0:b0 + nb]), by=16))
        mod_t = mod_columns(weigh_rows([mw_t[n]], which[n], nb), which[n], b0, nb)
    start_stream()
    wait(act, t_id)
    wait(dve, t_id)
    wait(act, latest("mw1 used"))
    mw_t = s_mw[1].mark(act.dma_start(MW[1][:, 0:MBLK], io["w_mod"][:, M_FIRST:M_FIRST + MBLK]), by=16)
    first_mw = mw_t.value
    feed()
    feed()

    def coef(n):
        return COEF[:, n * DB:(n + 1) * DB]

    def mod(n):
        return MOD[:, n * DB:(n + 1) * DB]

    def scaled(n, gain, m):
        return do(DV, [mod_t, t_vec], dve.scalar_tensor_tensor, out=coef(n), in0=mod(m), scalar=1.0,
                  in1=vec(gain), op0=ALU.add, op1=ALU.mult)

    def gated(n, gain, m, by):
        return do(DV, [mod_t, t_vec], dve.scalar_tensor_tensor, out=coef(n), in0=mod(m), scalar=by,
                  in1=vec(gain), op0=ALU.mult, op1=ALU.mult)

    c0 = scaled(0, "g_pre_ffn1", 1)
    wait(dve, c0, eps_t, ones_t)
    wait(act, eps_t)
    wait(pe, ones_t)
    a_t = prenorm([x_in] * DB, coef(0), mod(0))

    weighed = []

    def mod_weigh(i):
        dve.wait_ge(s_mw[1].sem, i * 16 + first_mw)
        weighed[:] = weigh_rows([], 1, MBLK)

    def mod_sum(i):
        nonlocal mod_t
        mod_t = mod_columns(weighed, 1, i * MBLK + M_FIRST, MBLK)

    def mod_load(i):
        wait(act, latest("mw1 used"))
        act.dma_start(MW[1][:, 0:MBLK], io["w_mod"][:, bass.ds(i * MBLK + (M_FIRST + MBLK), MBLK)]) \
            .then_inc(s_mw[1].sem, 16)

    def all_coefficients():
        gated(1, "g_post_ffn1", 2, 0.5)
        scaled(2, "g_pre_mix", 4)
        gated(3, "g_post_mix", 5, 1.0)
        scaled(4, "g_pre_ffn2", 7)
        gated(5, "g_post_ffn2", 8, 0.5)
        for n, gain in ((6, "ffn1_post_g_2"), (7, "ffn2_post_g_2")):
            t = do(DV, [], dve.tensor_scalar, coef(n), vec(gain), 0.5, None, ALU.mult)
        wait(dve, t)

    x_t = ffn(a_t, coef(1), between=(mod_weigh, mod_sum, mod_load), late=all_coefficients)
    a_t = prenorm(x_t, coef(2), mod(3))

    def const_into(dst, name, sem):
        c = CONST_AT[name]
        return sem.mark(act.dma_start(dst, io["consts"][:, c:c + dst.shape[-1]]), by=16)

    CQH, CQL = (sb(n, [P, 3, S], F32R, R + at) for n, at in (("CQH", 0), ("CQL", 6)))
    CKH, CKL = (sb(n, [P, 2, S], F32R, R + at) for n, at in (("CKH", 12), ("CKL", 16)))
    QKB = sb("QKB", [P, 12, S], F32, R + 20)
    VB = sb("VB", [P, 4, 768], F32, R + 44)
    COSQ, SINQ = sb("COSQ", [P, S], F32, R + 56), sb("SINQ", [P, S], F32, R + 58)
    SEL = sb("SEL", [P, 10 * P], F32, R + 60)
    ROTQ = sb("ROTQ", [P, P], F32, R + 65)
    INV = sb("INV", [P, 2], F32, R + 65.5)
    WID = sb("WID", [P, TT, H_IDX], F32, R + 65.5625)
    TOP8 = sb("TOP8", [P, 3, 8], F32, R + 65.75)
    STAT = sb("STAT", [P, 64], F32, R + 66)
    POSI, POSF = sb("POSI", [1, S], I32, R + 107), sb("POSF", [1, S], F32, R + 109)
    PICK = sb("PICK", [P, 6, P], F32, R + 67)
    COS16, SIN16, COS32, SIN32 = (sb(n, [P, S], F32, R + 70 + 2 * j)
                                  for j, n in enumerate(("COS16", "SIN16", "COS32", "SIN32")))
    QI, KI = sb("QI", [P, 2, S], F32, R + 78), sb("KI", [P, S], F32, R + 82)
    WORK = sb("WORK", [P, 9 * P], F32, R + 84)
    RL = sb("RL", [P, 2, S], F32, R + 89)
    MISC = sb("MISC", [P, S], F32, R + 93)
    XT = sb("XT", [P, 2, S], F32, R + 95)
    T1, T2 = sb("T1", [P, S], F32, R + 99), sb("T2", [P, S], F32, R + 101)
    RIN2 = sb("RIN2", [P, S], F32, R + 103)
    KRT = sb("KRT", [P, S], F32, R + 105)
    SQM = sb("SQM", [P, 2, S], F32, R + 84)

    s_c = [g.track(f"mixer1_{j}") for j in range(3)]
    wait(act, a_t[-1])
    pos_t = s_c[0].mark(act.dma_start(POSI[:, :], io["positions"]), by=16)
    const_into(INV[:, :], "inv", s_c[1])
    const_into(ROTQ[:, :], "rot_q", s_c[1])
    for j, name in enumerate(("rot32", "rot64", "pick_ki", "rot_ki", "pick_kr", "rot_kr")):
        const_t = const_into(PICK[:, j], name, s_c[1])
    ROT32, ROT64, PICK_KI, ROT_KI, PICK_KR, ROT_KR = (PICK[:, j] for j in range(6))

    wait(pe, *a_t)
    first_t = []
    for c in range(3):
        slot = take()
        first_t += [linear(2 * c + f, slot, f * P, 2 * P, A) for f in range(2)]
        used(first_t[-1])
        feed()
    misc_t = do(AC, [first_t[5]], act.activation, MISC[:, :], PS[:, 5], ACT.Copy)
    step("bank 5 read", misc_t)

    def small_norm(blocks, n, bank, out):
        mm = None
        wait(pe, latest(f"bank {bank} read"))
        for q, b in enumerate(blocks):
            wait(act, latest(f"sqm{q % 2} used"))
            s = do(AC, [first_t[b]], act.activation, SQM[:, q % 2], PS[:, b], ACT.Square)
            mm = do(PE, [s], pe.matmul, PS[:, bank], ONES[:, :], SQM[:, q % 2], start=q == 0,
                    stop=q == len(blocks) - 1)
            step(f"sqm{q % 2} used", mm)
            sq_last[b] = s
        return root_mean(bank, mm, n, out)

    sq_last = {}
    rq_t = small_norm([0, 1, 2], Q_LORA, 6, RIN[:, :])
    rk_t = small_norm([3, 4], KV_LORA, 7, RIN2[:, :])
    lora_t = []
    for b in range(5):
        r_t, r, gain, hi, lo, d = (rq_t, RIN, "g_cq", CQH, CQL, b) if b < 3 else (rk_t, RIN2, "g_ckv", CKH, CKL, b - 3)
        wait(dve, latest(f"xt{b % 2} used"))
        t = do(DV, [r_t, sq_last[b]], dve.scalar_tensor_tensor, out=XT[:, b % 2], in0=PS[:, b],
               scalar=vec(gain, d, 1), in1=r[:, :], op0=ALU.mult, op1=ALU.mult)
        step(f"bank {b} read", t)
        lora_t.append(split_from(XT[:, b % 2], hi[:, d], lo[:, d], [t]))
        step(f"xt{b % 2} used", lora_t[-1])
    CQ = [(CQH[:, k], CQL[:, k]) for k in range(3)]
    CK = [(CKH[:, k], CKL[:, k]) for k in range(2)]

    TURN = (6.28125, 0.0019350051879882812, 3.0199159819567529e-7)
    t = do(DV, [pos_t], dve.tensor_copy, POSF[:, :], POSI[:, :])
    wait(pe, latest("bank 7 read"))
    pos_t = do(PE, [t], pe.matmul, PS[:, 7], ONES[0:1, :], POSF[:, :], start=True, stop=True)
    ANG, TURNS = sb("ANG", [P, S], F32, R + 111), sb("TURNS", [P, S], I32, R + 113)
    TURNF, REST = sb("TURNF", [P, S], F32, R + 115), sb("REST", [P, 2, S], F32, R + 99)
    wait(dve, const_t)
    rest_free = [None, None]
    for j, (cos, sin) in enumerate(((COS16, SIN16), (COS32, SIN32))):
        t0 = do(DV, [pos_t], dve.tensor_scalar, ANG[:, :], PS[:, 7], INV[:, j:j + 1], None, ALU.mult)
        for n, (out, shift) in enumerate(((sin, 0.0), (cos, 0.25))):
            t = do(DV, [t0, rest_free[n]], dve.tensor_scalar, TURNS[:, :], ANG[:, :], 1.0 / (2 * math.pi), shift, ALU.mult, ALU.add)
            t = do(DV, [t], dve.tensor_copy, TURNF[:, :], TURNS[:, :])
            src = ANG[:, :]
            for part in TURN:
                t = do(DV, [t], dve.scalar_tensor_tensor, out=REST[:, n], in0=TURNF[:, :], scalar=-part,
                       in1=src, op0=ALU.mult, op1=ALU.add)
                src = REST[:, n]
            t = do(DV, [t], dve.tensor_scalar, REST[:, n], REST[:, n], shift * 2 * math.pi, None, ALU.add)
            t = do(DV, [t], dve.tensor_scalar, REST[:, n], REST[:, n], 3.1415925, -3.1415925, ALU.min, ALU.max)
            rest_free[n] = do(AC, [t], act.activation, out[:, :], REST[:, n], ACT.Sin)
    step("bank 7 read", t0)
    wait(dve, rest_free[1])
    table_t = do(DV, [rest_free[1]], dve.memset, SINQ[0:NOPE, :], 0.0)
    do(DV, [], dve.memset, COSQ[0:NOPE, :], 1.0)
    do(DV, [], dve.tensor_copy, COSQ[NOPE:D_QK, :], COS16[NOPE:D_QK, :])
    table_t = do(DV, [], dve.tensor_copy, SINQ[NOPE:D_QK, :], SIN16[NOPE:D_QK, :])

    def rotate(x, x_t, rot_w, bank, cos, sin, out, rows=slice(0, P), before=(), rhs=None, n=P):
        wait(pe, latest(f"bank {bank} read"))
        mm = do(PE, [x_t, const_t], pe.matmul, PS[0:n, bank], rot_w, x if rhs is None else rhs, start=True, stop=True)
        wait(dve, latest("t12 used"))
        a = do(DV, [x_t, table_t, mm, *before], dve.tensor_tensor, T1[rows, :], x[rows, :], cos[rows, :], ALU.mult)
        b = do(DV, [], dve.tensor_tensor, T2[rows, :], PS[rows, bank], sin[rows, :], ALU.mult)
        step(f"bank {bank} read", b)
        c = do(DV, [a, b], dve.tensor_tensor, out, T1[rows, :], T2[rows, :], ALU.add)
        step("t12 used", c)
        return c

    slot = take()
    wait(pe, *lora_t)
    qi_t = []
    iq = [linear(f, slot, f * P, 2 * P, CQ) for f in range(2)]
    used(iq[1])
    for f in range(2):
        wait(act, latest(f"xt{f} used"))
        t = do(AC, [iq[f]], act.activation, XT[:, f], PS[:, f], ACT.Copy)
        step(f"bank {f} read", t)
        qi_t.append(rotate(XT[:, f], t, ROT32, 2 + f, COS16, SIN16, QI[:, f]))
        step(f"xt{f} used", qi_t[-1])
    feed()
    wait(pe, latest("bank 4 read"))
    t = do(PE, [misc_t, const_t], pe.matmul, PS[:, 4], PICK_KI, MISC[:, :], start=True, stop=True)
    ki_t = rotate(PS[:, 4], t, ROT_KI, 5, COS16, SIN16, KI[:, :], rhs=MISC[:, :])
    step("bank 4 read", ki_t)
    wait(pe, latest("bank 6 read"))
    t = do(PE, [], pe.matmul, PS[:, 6], PICK_KR, MISC[:, :], start=True, stop=True)
    kr_t = rotate(PS[:, 6], t, ROT_KR, 7, COS16, SIN16, KRT[NOPE:D_QK, :], rows=slice(NOPE, D_QK), rhs=MISC[:, :])
    step("bank 6 read", kr_t)
    wait(pe, latest("bank 5 read"))
    for i in range(TT):
        t = pe.transpose(PS[:, 5, i * P:(i + 1) * P], MISC[:, i * P:(i + 1) * P], IDENT[:, :])
    t = PE.mark(t)
    wid_t = do(AC, [t], act.activation, WID[:, :, :],
               PS[:, 5].rearrange("p (i c) -> p i c", i=TT)[:, :, 64:64 + H_IDX], ACT.Copy, scale=H_IDX ** -0.5)
    step("bank 5 read", wid_t)

    def tile_cols(i):
        at = (0, 2 * P, 5 * P)[i - 1]
        return slice(at, at + (i + 1) * P)

    wait(pe, *qi_t, ki_t)
    work_t, n_u = {}, 0
    for h in range(H_IDX):
        rows = slice(32 * (h % 4), 32 * (h % 4) + 32)
        for i in range(1, TT):
            n, bank = (i + 1) * P, n_u % 4
            wait(pe, latest(f"bank {bank} read"))
            mm = do(PE, [], pe.matmul, PS[:, bank, 0:n], QI[rows, h // 4, i * P:(i + 1) * P],
                    KI[rows, 0:n], start=True, stop=True)
            wait(act, latest(f"rl{n_u % 2} used"))
            r = do(AC, [mm], act.activation, RL[:, n_u % 2, 0:n], PS[:, bank, 0:n], ACT.Relu, scale=32 ** -0.5)
            step(f"bank {bank} read", r)
            dst, wcol = WORK[:, tile_cols(i)], WID[:, i, h:h + 1]
            if h == 0:
                work_t[i] = do(DV, [r, wid_t, latest("sqm0 used"), latest("sqm1 used")],
                               dve.tensor_scalar, dst, RL[:, n_u % 2, 0:n], wcol, None, ALU.mult)
            else:
                work_t[i] = do(DV, [r, work_t[i]], dve.scalar_tensor_tensor, out=dst, in0=RL[:, n_u % 2, 0:n],
                               scalar=wcol, in1=dst, op0=ALU.mult, op1=ALU.add)
            step(f"rl{n_u % 2} used", work_t[i])
            n_u += 1
    STRUCK = -3e38
    for i in range(1, TT):
        diag = WORK[:, tile_cols(i)][:, i * P:(i + 1) * P]
        work_t[i] = do(DV, [work_t[i]], dve.tensor_tensor, diag, diag, CAUSAL[:, :], ALU.add)
    for _ in range(TOPK // 8):
        for i in range(1, TT):
            src = WORK[:, tile_cols(i)]
            work_t[i] = do(DV, [work_t[i]], dve.max, TOP8[:, i - 1], src)
        for i in range(1, TT):
            src = WORK[:, tile_cols(i)]
            work_t[i] = do(DV, [work_t[i]], dve.match_replace, src, TOP8[:, i - 1], src, STRUCK)
    do(DV, [], dve.tensor_copy, SEL[:, 0:P], CAUSAL[:, :])
    for i in range(1, TT):
        src = WORK[:, tile_cols(i)]
        at = tile_cols(i).start + P
        sel_t = do(DV, [work_t[i]], dve.tensor_scalar, SEL[:, at:at + (i + 1) * P], src, -2e38, NEG,
                   ALU.is_gt, ALU.mult)

    wait(pe, AC.now())
    with wloop(3, 2) as i:
        for c in range(2):
            slot = take()
            mm = [linear(4 + 2 * c + f, slot, f * P, 2 * P, A) for f in range(2)]
            used(mm[1])
            for f in range(2):
                qkb_t = do(AC, [mm[f]], act.activation,
                           QKB[:, bass.ds(i * 4 + (2 * c + f), 1)].rearrange("p a s -> p (a s)"),
                           PS[:, 4 + 2 * c + f], ACT.Copy)
                step(f"bank {4 + 2 * c + f} read", qkb_t)
            feed()
    vb_t = []
    for c in range(3):
        slot = take()
        for r in range(4):
            bank = (4 * c + r) % 8
            wait(pe, latest(f"bank {bank} read"))
            m, n = None, 0
            for k in range(DB):
                cols = slice(k * 256, (k + 1) * 256)
                for wt, x in ((WHI, AHI), (WHI, ALO), (WLO, AHI)):
                    m = pe.matmul(PS[:, bank, 0:256], x[:, k, r::4], wt[:, slot, cols], start=n == 0, stop=n == 23)
                    n += 1
            mm = PE.mark(m)
            t = do(AC, [mm], act.activation, VB[:, r, c * 256:(c + 1) * 256], PS[:, bank, 0:256], ACT.Copy)
            step(f"bank {bank} read", t)
            vb_t = [t]
        used(mm)
        feed()
    wait(pe, qkb_t, table_t)
    wait(dve, qkb_t)
    meet()
    with g.loop(6) as i:
        for f in range(2):
            blk = QKB[:, bass.ds(i * 2 + f, 1)].rearrange("p a s -> p (a s)")
            wait(pe, latest(f"bank {f} read"))
            mm = do(PE, [], pe.matmul, PS[:, f], ROT64, blk, start=True, stop=True)
            wait(dve, latest("t12 used"))
            a = do(DV, [mm], dve.tensor_tensor, T1[:, :], blk, COS32[:, :], ALU.mult)
            b = do(DV, [], dve.tensor_tensor, T2[:, :], PS[:, f], SIN32[:, :], ALU.mult)
            step(f"bank {f} read", b)
            qkr_t = do(DV, [a, b], dve.tensor_tensor, blk, T1[:, :], T2[:, :], ALU.add)
            step("t12 used", qkr_t)

    QF, KF = sb("QF", [P, 2, S], F32, R + 67), sb("KF", [P, 2, S], F32, R + 71)
    VP = sb("VP", [P, TT, P], F32, R + 75)
    SM = sb("SM", [P, 2, 10 * P], F32, R + 77)
    PT = sb("PT", [P, TT, S], F32, R + 87)
    OAH, OAL = sb("OAH", [P, 4, S], F32R, R + 103), sb("OAL", [P, 4, S], F32R, R + 111)
    wait(dve, kr_t, sel_t, qkr_t.last())
    for a in range(2):
        kf_t = do(DV, [], dve.tensor_copy, KF[NOPE:D_QK, a], KRT[NOPE:D_QK, :])
    phase2_t = kf_t
    wait(act, phase2_t)


    def causal_softmax(SM, STAT, head, q, k, mask, scale, banks, waits, mask_t=(), key_bias=None):
        col, st = 0, STAT[:, head * 32:(head + 1) * 32]
        low, sums, inv = st[:, 0:4], st[:, 4:8], st[:, 8:12]
        wait(dve, latest(f"sm{head} used"))
        parts = []
        for i in range(TT):
            n = (i + 1) * P
            wait(pe, latest(f"bank {banks[i]} read"))
            mm = do(PE, waits, pe.matmul, PS[:, banks[i], 0:n], q[:, i * P:(i + 1) * P], k[:, 0:n], start=True,
                    stop=key_bias is None)
            if key_bias:
                mm = do(PE, [], pe.matmul, PS[:, banks[i], 0:n], key_bias[0], key_bias[1][:, 0:n], start=False,
                        stop=True)
            sm = SM[:, head, col:col + n]
            do(DV, [mm, *mask_t], dve.memset, st[:, 12 + i:13 + i], 0.0)
            t = do(DV, [], dve.tensor_tensor_reduce, sm, PS[:, banks[i], 0:n], mask[:, col:col + n], -scale,
                   3e38, ALU.add, ALU.min, low[:, i:i + 1])
            step(f"bank {banks[i]} read", t)
            e = do(AC, [t], act.activation, sm, sm, ACT.Exp, bias=low[:, i:i + 1], scale=-1.0,
                   accum_out=sums[:, i:i + 1])
            parts.append((e, sm, n, col))
            col += n
        r = None
        for i, (e, sm, n, c) in enumerate(parts):
            r = do(DV, [e], dve.reciprocal, inv[:, i:i + 1], sums[:, i:i + 1])
            parts[i] = (do(DV, [r], dve.tensor_scalar, sm, sm, inv[:, i:i + 1], None, ALU.mult), sm, n, c)
        return parts

    def transposed(PT, parts, banks, head):
        wait(act, latest("pt used"))
        for i, (t, sm, n, c) in enumerate(parts):
            wait(pe, latest(f"bank {banks[i]} read"))
            wait(pe, t)
            for j in range(i + 1):
                m = pe.transpose(PS[:, banks[i], j * P:(j + 1) * P], sm[:, j * P:(j + 1) * P], IDENT[:, :])
            m = PE.mark(m)
            pt_t = do(AC, [m], act.activation, PT[:, 0:i + 1, i * P:(i + 1) * P],
                      PS[:, banks[i], 0:n].rearrange("p (j q) -> p j q", q=P), ACT.Copy)
            step(f"bank {banks[i]} read", pt_t)
        step(f"sm{head} used", m)
        return pt_t

    def weighted_values(PT, out, v, pt_t, v_t):
        wait(pe, pt_t, v_t)
        for j in range(TT):
            m = pe.matmul(out[:, j * P:S], v[j], PT[:, j, j * P:S], start=j == 0, stop=j == TT - 1)
        m = PE.mark(m)
        step("pt used", m)
        return m

    meet()
    with wloop(2, 2) as i:
        for pair in range(2):
            slot = take()
            q_mm = [linear(f, slot, f * D_QK, 2 * D_QK, CQ, width=D_QK, rows=D_QK) for f in range(2)]
            k_mm = linear(2, slot, 576, P, CK)
            wait(pe, latest("bank 3 read"))
            for t in range(TT):
                n = 0
                for k in range(2):
                    for wt, x in ((WHI, CKH), (WHI, CKL), (WLO, CKH)):
                        m = pe.matmul(PS[:, 3, t * P:(t + 1) * P], x[:, k, t * P:(t + 1) * P],
                                      wt[:, slot, 832 + k * P:832 + (k + 1) * P], start=n == 0, stop=n == 5)
                        n += 1
            v_mm = PE.mark(m)
            used(v_mm)
            for f in range(2):
                wait(act, latest(f"kf{f} used"))
                k_t = do(AC, [k_mm], act.activation, KF[0:NOPE, f], PS[f * NOPE:(f + 1) * NOPE, 2], ACT.Copy)
            step("bank 2 read", k_t)
            q_t = []
            for f in range(2):
                wait(act, latest(f"xt{f} used"))
                t = do(AC, [q_mm[f]], act.activation, XT[0:D_QK, f], PS[0:D_QK, f], ACT.Copy)
                step(f"bank {f} read", t)
                wait(dve, latest(f"qf{f} used"))
                q_t.append(rotate(XT[:, f], t, ROTQ[0:D_QK, 0:D_QK], 4 + f, COSQ, SINQ, QF[0:D_QK, f],
                                  rows=slice(0, D_QK), rhs=XT[0:D_QK, f], n=D_QK))
                step(f"xt{f} used", q_t[-1])
            wait(act, latest("vp used"))
            v_t = do(AC, [v_mm], act.activation, VP[:, :, :], PS[:, 3].rearrange("p (t c) -> p t c", c=P), ACT.Copy)
            step("bank 3 read", v_t)
            feed()
            parts = []
            for f in range(2):
                banks = ((6, 7, 0, 1), (2, 3, 4, 5))[f]
                parts.append(causal_softmax(SM, STAT, f, QF[0:D_QK, f], KF[0:D_QK, f], SEL, D_QK ** -0.5, banks,
                                            [q_t[f], k_t, kf_t]))
                step(f"qf{f} used", PE.now())
                step(f"kf{f} used", PE.now())
            wait(pe, latest("bank 0 read"))
            for f in range(2):
                pt_t = transposed(PT, parts[f], ((6, 7, 1, 2), (3, 4, 5, 6))[f], f)
                o_mm = weighted_values(PT, PS[f * NOPE:(f + 1) * NOPE, 0], [VP[:, j, f * NOPE:(f + 1) * NOPE] for j in range(TT)],
                                       pt_t, v_t)
            step("vp used", o_mm)
            blk = bass.ds(i * 2 + pair, 1)
            t = do(AC, [o_mm], act.activation, OAH[:, blk].rearrange("p a s -> p (a s)"), PS[:, 0], ACT.Copy)
            oa_t = do(DV, [t], dve.tensor_tensor, OAL[:, blk].rearrange("p a s -> p (a s)"), PS[:, 0],
                      OAH[:, blk].rearrange("p a s -> p (a s)").bitcast(F32), ALU.subtract)
            step("bank 0 read", oa_t)

    MASKB = sb("MASKB", [P, 9, P], F32, R + 67)
    SMB = sb("SMB", [P, 2, 6 * P], F32, R + 77)
    PTB = sb("PTB", [P, 2, 6 * P], F32, R + 87)
    OBH, OBL = sb("OBH", [P, 2, S], F32R, R + 0), sb("OBL", [P, 2, S], F32R, R + 4)
    phase3 = [oa_t.last(), o_mm.last()]
    wait(act, *phase3)
    wait(dve, *phase3)
    c = CONST_AT["near0"]
    mask_t = s_c[2].mark(act.dma_start(MASKB[:, :, :], io["consts"][:, c:c + 9 * P].rearrange("p (m k) -> p m k", k=P)), by=16)
    wait(pe, qkr_t.last(), *vb_t)
    n_u = 0
    for hp in range(2):
        wait(pe, latest("bank 7 read"))
        for r in range(4):
            for f in range(2):
                u = n_u % 2
                h, rows = 2 * hp + f, slice(f * 64, f * 64 + 64)
                b0, b1, bt = 2 * u, 2 * u + 1, 4 + u
                st = STAT[:, 32 * u:32 * u + 32]

                def q_of(grp):
                    return QKB[rows, 2 * grp + hp, r::4]

                def k_of(grp, res):
                    return QKB[rows, 6 + 2 * grp + hp, res::4]

                wait(pe, latest(f"bank {b0} read"), latest(f"bank {b1} read"))
                for j in range(4):
                    m = pe.matmul(PS[:, b0, j * P:(j + 1) * P], q_of(0), k_of(0, j), start=True, stop=True)
                for grp in (1, 2):
                    m = pe.matmul(PS[:, b1, (grp - 1) * P:grp * P], q_of(grp), k_of(grp, r), start=True, stop=True)
                mm = PE.mark(m)
                wait(dve, latest(f"smb{u} used"))
                t = do(DV, [mm, mask_t], dve.tensor_tensor_reduce, SMB[:, u, 0:S], PS[:, b0],
                       MASKB[:, 3 - r:7 - r].rearrange("p m k -> p (m k)"), -0.125, 3e38, ALU.add, ALU.min, st[:, 0:1])
                step(f"bank {b0} read", t)
                t = do(DV, [t], dve.tensor_tensor_reduce, SMB[:, u, S:S + 2 * P], PS[:, b1, 0:2 * P],
                       MASKB[:, 7:9].rearrange("p m k -> p (m k)"), -0.125, st[:, 0:1], ALU.add, ALU.min, st[:, 1:2])
                step(f"bank {b1} read", t)
                e = do(AC, [t], act.activation, SMB[:, u], SMB[:, u], ACT.Exp, bias=st[:, 1:2], scale=-1.0,
                       accum_out=st[:, 2:3])
                t = do(DV, [e], dve.reciprocal, st[:, 3:4], st[:, 2:3])
                p_t = do(DV, [t], dve.tensor_scalar, SMB[:, u], SMB[:, u], st[:, 3:4], None, ALU.mult)
                wait(pe, latest(f"bank {bt} read"))
                wait(pe, p_t)
                for j in range(4):
                    m = pe.transpose(PS[:, bt, j * P:(j + 1) * P], SMB[:, u, j * P:(j + 1) * P], IDENT[:, :])
                m = PE.mark(m)
                wait(act, latest(f"ptb{u} used"))
                t = do(AC, [m], act.activation, PTB[:, u, 0:S], PS[:, bt], ACT.Copy)
                wait(pe, latest("bank 6 read"))
                for j in range(2):
                    m = pe.transpose(PS[:, 6, j * P:(j + 1) * P], SMB[:, u, S + j * P:S + (j + 1) * P], IDENT[:, :])
                m = PE.mark(m)
                step(f"smb{u} used", m)
                step(f"bank {bt} read", t)
                t = do(AC, [m], act.activation, PTB[:, u, S:S + 2 * P], PS[:, 6, 0:2 * P], ACT.Copy)
                step("bank 6 read", t)
                wait(pe, t)
                for j in range(6):
                    grp, res = (0, j) if j < 4 else (j - 3, r)
                    c = grp * 256 + h * 64
                    m = pe.matmul(PS[f * 64:f * 64 + 64, 7, r * P:(r + 1) * P], VB[:, res, c:c + 64],
                                  PTB[:, u, j * P:(j + 1) * P], start=j == 0, stop=j == 5)
                o_mm = PE.mark(m)
                step(f"ptb{u} used", o_mm)
                n_u += 1
        src = PS[:, 7].rearrange("p (r a) -> p a r", r=4)
        dst = [x[:, hp].rearrange("p (a r) -> p a r", r=4) for x in (OBH, OBL)]
        t = do(AC, [o_mm], act.activation, dst[0], src, ACT.Copy)
        ob_t = do(DV, [t], dve.tensor_tensor, dst[1], src, dst[0].bitcast(F32), ALU.subtract)
        step("bank 7 read", ob_t)
    OA = [(OAH[:, k], OAL[:, k]) for k in range(4)]
    OB = [(OBH[:, k], OBL[:, k]) for k in range(2)]

    ZH, ZL = sb("ZH", [P, DB, S], F32R, R + 20), sb("ZL", [P, DB, S], F32R, R + 36)
    SG = sb("SG", [P, 2, S], F32, R + 77)
    TZ = sb("TZ", [P, 2, S], F32, R + 81)
    def gated_sum(n, a_in, rhs_a, rhs_b, b_at, SG, TZ, ZH, ZL, gate_bias=None):
        meet()
        with wloop(n, 2) as i:
            slot = take()
            gate_mm = [linear(f, slot, f * D, P, a_in) for f in range(2)]
            used(gate_mm[1])
            sg_t = []
            for f in range(2):
                wait(act, latest(f"sg{f} used"))
                bias = 0.0 if gate_bias is None else VEC[:, bass.ds(i + (gate_bias + f * DB), 1)]
                sg_t.append(do(AC, [gate_mm[f]], act.activation, SG[:, f], PS[:, f], ACT.Sigmoid, bias=bias))
                step(f"bank {f} read", sg_t[f])
            feed()
            slot = take()
            ua = linear(2, slot, 0, P, rhs_a)
            ub = linear(3, slot, b_at, P, rhs_b)
            used(ub)
            t = []
            for f, mm in enumerate((ua, ub)):
                wait(dve, latest(f"tz{f} used"))
                t.append(do(DV, [mm, sg_t[f]], dve.tensor_tensor, TZ[:, f], PS[:, 2 + f], SG[:, f], ALU.mult))
                step(f"bank {2 + f} read", t[f])
                step(f"sg{f} used", t[f])
            s = do(DV, t, dve.tensor_tensor, TZ[:, 0], TZ[:, 0], TZ[:, 1], ALU.add)
            step("tz1 used", s)
            blk = bass.ds(i, 1)
            h = do(AC, [s], act.activation, ZH[:, blk], TZ[:, 0:1], ACT.Copy)
            z_t = do(DV, [h], dve.tensor_tensor, ZL[:, blk], TZ[:, 0:1], ZH[:, blk].bitcast(F32), ALU.subtract)
            step("tz0 used", z_t)
            feed()
        return z_t

    wait(act, ob_t)
    wait(pe, oa_t.last(), ob_t)
    z_t = gated_sum(DB, A, OA, OB, 4 * P, SG, TZ, ZH, ZL)

    def square_linear(rhs, ready, sq_at, y_at):
        u = g.next_name()
        Y, SQ = sb(f"Y{u}", [P, DB, S], F32, R + y_at), sb(f"SQ{u}", [P, 2, S], F32, R + sq_at)
        wait(pe, *ready)
        wait(act, *ready)
        wait(dve, *ready)
        y_t, ssq = [], None
        for c in range(4):
            slot = take()
            for f in range(2):
                d = 2 * c + f
                mm = linear(d, slot, f * P, 2 * P, rhs)
                t, ssq = take_output(Y, SQ, d, d, mm, ssq)
                y_t.append(t)
            used(mm)
            feed()
        return Y, y_t, ssq

    Z = [(ZH[:, k], ZL[:, k]) for k in range(DB)]
    Y, y_t, ssq = square_linear(Z, [z_t.last()], 88, 98)
    x_t = residual(Y, y_t, ssq, 0, coef(3))
    a_t = prenorm(x_t, coef(4), mod(6))
    x_t = ffn(a_t, coef(5))
    a_t = prenorm(x_t, vec("ffn1_pre_g_2"))
    x_t = ffn(a_t, coef(6))

    OBH2, OBL2 = sb("OBH2", [P, DB, S], F32R, R), sb("OBL2", [P, DB, S], F32R, R + 16)
    OAR = sb("OAR", [P, HG, S], F32, R + 32)
    FQ, FK, FVF = (sb(n, [P, S], F32, R + 48 + 2 * j) for j, n in enumerate(("FQ", "FK", "FVF")))
    FV = sb("FV", [P, TT, P], F32, R + 54)
    MASKC = sb("MASKC", [P, 10 * P], F32, R + 56)
    NEGC, PICKH = sb("NEGC", [P, S], F32, R + 61), sb("PICKH", [P, P], F32, R + 63)
    LEVELS = sb("LEVELS", [P, 8, P], F32, R + 64)
    RESET = sb("RESET", [P, S], F32, R + 68)
    XC, SIG = sb("XC", [P, 2, S], F32, R + 70), sb("SIG", [P, 2, S], F32, R + 74)
    XG, SIGG, GS, QH, KK, FG, LF, B = (sb(n, [P, S], F32, R + 78 + 2 * j) for j, n in
                                       enumerate(("XG", "SIGG", "GS", "QH", "KK", "FG", "LF", "B")))
    E = sb("E", [P, 3, S], F32, R + 94)
    KS, QS, IFM = (sb(n, [P, S], F32, R + 100 + 2 * j) for j, n in enumerate(("KS", "QS", "IFM")))
    ITM, KST = sb("ITM", [P, TT, P], F32, R + 106), sb("KST", [P, TT, P], F32, R + 108)
    STATE = sb("STATE", [P, TT - 1, P], F32, R + 110)
    PAIRS = sb("PAIRS", [P, TT, P], F32, R + 112)
    SQO = sb("SQO", [P, 2, S], F32, R + 114)
    DEC, SCR = sb("DEC", [P, TT], F32, R + 118), sb("SCR", [P, 32], F32, R + 118.125)
    LB, OML = sb("LB", [P, HG], F32, R + 118.25), sb("OML", [P, HG], F32, R + 118.3125)
    FBIAS = sb("FBIAS", [P, 1], F32, R + 118.375)

    s_c2 = [g.track(f"mixer2_{j}") for j in range(2)]
    wait(act, x_t[-1])
    const_into(LEVELS[:, :, :].rearrange("p a b -> p (a b)"), "levels", s_c2[0])
    const_into(RESET[:, :], "reset", s_c2[0])
    const2_t = s_c2[0].mark(act.dma_start(FBIAS[0:FOX, :], io["fox_bias"]), by=16)
    a_t = prenorm(x_t, vec("mix_pre_g_2"))
    wait(act, a_t[-1])
    wait(dve, const2_t)

    wait(pe, *a_t)
    slot = take()
    fb_mm = linear(0, slot, 0, P, A)
    used(fb_mm)
    feed()
    x_f, low_f, t_f = E[0:FOX, 0], E[0:FOX, 1], E[0:FOX, 2]
    t = do(DV, [fb_mm], dve.tensor_scalar, x_f, PS[0:FOX, 0], FBIAS[0:FOX, :], None, ALU.add)
    step("bank 0 read", t)
    t = do(DV, [t], dve.tensor_scalar, low_f, x_f, 0.0, None, ALU.min)
    t = do(DV, [t], dve.scalar_tensor_tensor, out=t_f, in0=low_f, scalar=2.0, in1=x_f, op0=ALU.mult, op1=ALU.subtract)
    t = do(AC, [t], act.activation, t_f, t_f, ACT.Exp)
    t = do(AC, [t], act.activation, t_f, t_f, ACT.Ln, bias=ONES[0:FOX, 0:1])
    t = do(DV, [t], dve.tensor_tensor, x_f, low_f, t_f, ALU.subtract)
    s = do(DV, [t], dve.memset, t_f, 1.0)
    t = do(DV, [t, s], dve.tensor_tensor_scan, low_f, t_f, x_f, 0.0, ALU.mult, ALU.add)
    negc_t = do(DV, [t], dve.tensor_scalar, NEGC[0:FOX, :], low_f, -math.sqrt(P), None, ALU.mult)

    t = do(DV, [], dve.tensor_tensor, LB[:, :], vec("hg_lb_logits_2", DB), vec("hg_lb_logits_2"), ALU.subtract)
    t = do(AC, [t], act.activation, LB[:, :], LB[:, :], ACT.Exp)
    t = do(DV, [t], dve.tensor_scalar, LB[:, :], LB[:, :], 1.0, None, ALU.add)
    t = do(DV, [t], dve.reciprocal, LB[:, :], LB[:, :])
    t = do(DV, [t], dve.tensor_scalar, OML[:, :], LB[:, :], -1.0, 1.0, ALU.mult, ALU.add)
    do(DV, [], dve.memset, SSQ[:, :], 0.0)
    t = do(DV, [], dve.memset, PAIRS[:, :, :], 0.0)
    wait(dve, t, negc_t)
    wait(act, t, negc_t)

    settled = [0]

    def settle(*waits):
        settled[0] += 1
        do(DV, waits, dve.memset, SCR[:, settled[0] % 32:settled[0] % 32 + 1], 0.0)

    def projection(banks, slot):
        marks = []

        def work():
            for f, bank in enumerate(banks):
                wait(pe, latest(f"bank {bank} read"))
                for q in range(DB):
                    at = q * 2 * P + f * P
                    for r, (wt, x) in enumerate(((WHI, A[q][0]), (WHI, A[q][1]), (WLO, A[q][0]))):
                        m = pe.matmul(PS[:, bank], wt[:, slot, at:at + P], x, start=q == 0 and r == 0,
                                      stop=q == DB - 1 and r == 2)
                        if q == DB - 1 and r == 2:
                            marks.append(PE.mark(m))
                            if f:
                                used(marks[1])
                        yield

        steps = work()

        def run(n=2 * 3 * DB + 1):
            for _ in range(n):
                next(steps, None)

        return run, marks

    FLOOR = -80.0

    def sigmoid(out, x, waits):
        t = do(AC, waits, act.activation, out, x, ACT.Exp, scale=-1.0)
        t = do(AC, [t], act.activation, out, out, ACT.Ln, bias=ONES[:, 0:1])
        return do(AC, [t], act.activation, out, out, ACT.Exp, scale=-1.0)

    def take_qf(marks):
        wait(dve, latest("xc used"))
        t = do(DV, marks, dve.tensor_scalar, XC[:, :, :], PS[:, 4:6], FLOOR, None, ALU.max)
        step("bank 4 read", t)
        step("bank 5 read", t)
        step("xc ready", t)

    def hgrn_head(h, last):
        slot = take()
        ig = [linear(f, slot, f * P, 2 * P, A) for f in range(2)]
        used(ig[1])
        feed()
        wait(act, latest("xc ready"), latest("sig used"))
        t = sigmoid(SIG[:, :, :], XC[:, :, :], [])
        wait(dve, latest("qk used"))
        q_t = do(DV, [t], dve.tensor_tensor, QH[:, :], XC[:, 0], SIG[:, 0], ALU.mult)
        step("xc used", q_t)
        t = do(DV, [], dve.tensor_scalar, FG[:, :], SIG[:, 1], OML[:, bass.ds(h, 1)], LB[:, bass.ds(h, 1)], ALU.mult, ALU.add)
        step("sig used", t)
        k_t = do(DV, [t], dve.tensor_scalar, KK[:, :], FG[:, :], -1.0, 1.0, ALU.mult, ALU.add)
        t = do(AC, [t], act.activation, LF[:, :], FG[:, :], ACT.Ln)
        b_t = do(DV, [t], dve.tensor_tensor_scan, B[:, :], RESET[:, :], LF[:, :], 0.0, ALU.mult, ALU.add)
        b4 = B[:, :].rearrange("p (c s) -> p c s", s=P)
        wait(dve, latest("ks used"))
        t = do(DV, [b_t], dve.tensor_tensor, KS[:, :].rearrange("p (c s) -> p c s", s=P),
               b4[:, :, P - 1:P].to_broadcast([P, TT, P]), b4, ALU.subtract)
        t = do(AC, [t], act.activation, KS[:, :], KS[:, :], ACT.Exp)
        ks_t = do(DV, [t, k_t], dve.tensor_tensor, KS[:, :], KS[:, :], KK[:, :], ALU.mult)
        wait(act, latest("qs used"))
        do(AC, [], act.activation, DEC[:, :].rearrange("p (c a) -> p c a", a=1), b4[:, :, P - 1:P], ACT.Exp)
        t = do(AC, [], act.activation, QS[:, :], B[:, :], ACT.Exp)
        qs_t = do(DV, [t, q_t], dve.tensor_tensor, QS[:, :], QS[:, :], QH[:, :], ALU.mult)
        wait(act, latest("ifm used"))
        i_t = do(AC, [ig[0]], act.activation, IFM[:, :], PS[:, 0], ACT.Copy)
        step("bank 0 read", i_t)
        wait(dve, latest("gs used"))
        t = do(DV, [ig[1]], dve.tensor_scalar, XG[:, :], PS[:, 1], FLOOR, None, ALU.max)
        step("bank 1 read", t)
        t = sigmoid(SIGG[:, :], XG[:, :], [t])
        gs_t = do(DV, [t], dve.tensor_tensor, GS[:, :], XG[:, :], SIGG[:, :], ALU.mult)

        if last:
            run, marks = (lambda n=0: None), None
        else:
            slot = take()
            run, marks = projection((4, 5), slot)

        def pairs(n, left, right, waits):
            bank = 6 + n % 2
            wait(pe, latest(f"bank {bank} read"))
            wait(pe, *waits)
            for c in range(TT):
                m = pe.matmul(PS[:, bank, c * P:(c + 1) * P], left[:, c * P:(c + 1) * P],
                              right[:, c * P:(c + 1) * P], start=True, stop=True)
            return PE.mark(m)

        def keep(n, mm, before):
            settle(mm, before)
            t = do(DV, [], dve.copy_predicated, PAIRS[:, :, :],
                   LEVELS[:, n:n + 1].bitcast(mybir.dt.uint32).to_broadcast([P, TT, P]),
                   PS[:, 6 + n % 2].rearrange("p (c t) -> p c t", t=P))
            step(f"bank {6 + n % 2} read", t)
            return t

        wait(dve, latest("pairs used"))
        mm = pairs(0, KK[:, :], QH[:, :], [q_t, k_t])
        run(6)
        wait(pe, latest("bank 2 read"), latest("bank 3 read"))
        wait(pe, ks_t)
        for c in range(TT - 1):
            m = pe.transpose(PS[:, 2, c * P:(c + 1) * P], KS[:, c * P:(c + 1) * P], IDENT[:, :])
        t = PE.mark(m)
        step("ks used", t)
        wait(act, latest("kst used"))
        kst_t = do(AC, [t], act.activation, KST[:, 0:TT - 1], PS[:, 2, 0:(TT - 1) * P].rearrange("p (c t) -> p c t", t=P), ACT.Copy)
        step("bank 2 read", kst_t)
        wait(pe, i_t)
        for c in range(TT):
            m = pe.transpose(PS[:, 3, c * P:(c + 1) * P], IFM[:, c * P:(c + 1) * P], IDENT[:, :])
        t = PE.mark(m)
        step("ifm used", t)
        wait(act, latest("itm used"))
        it_t = do(AC, [t], act.activation, ITM[:, :, :], PS[:, 3].rearrange("p (c t) -> p c t", t=P), ACT.Copy)
        step("bank 3 read", it_t)

        kept = keep(0, mm, q_t)
        e_t, mm, exp_t = {}, {}, {}
        for n in range(1, 10):
            if n < 8:
                half = 1 << (n - 1)
                bl = B[:, :].rearrange("p (m two l) -> p m two l", two=2, l=half)
                el = E[:, n % 3].rearrange("p (m two l) -> p m two l", two=2, l=half)
                anchor = bl[:, :, 0, half - 1:half].to_broadcast([P, S // (2 * half), half])
                wait(dve, latest(f"e{n % 3} used"))
                do(DV, [b_t], dve.tensor_tensor, el[:, :, 0], anchor, bl[:, :, 0], ALU.subtract)
                t = do(DV, [], dve.tensor_tensor, el[:, :, 1], bl[:, :, 1], anchor, ALU.subtract)
                exp_t[n] = do(AC, [t], act.activation, E[:, n % 3], E[:, n % 3], ACT.Exp)
            if 0 < n - 1 < 8:
                o, half = n - 1, 1 << (n - 2)
                el, kl, ql = (x.rearrange("p (m two l) -> p m two l", two=2, l=half)
                              for x in (E[:, o % 3], KK[:, :], QH[:, :]))
                do(DV, [exp_t[o], k_t], dve.tensor_tensor, el[:, :, 0], el[:, :, 0], kl[:, :, 0], ALU.mult)
                t = do(DV, [], dve.tensor_tensor, el[:, :, 1], el[:, :, 1], ql[:, :, 1], ALU.mult)
                mm[o] = pairs(o, E[:, o % 3], E[:, o % 3], [t])
                step(f"e{o % 3} used", mm[o])
                run(6)
            if 0 < n - 2 < 8:
                kept = keep(n - 2, mm[n - 2], kept)
            if n == 4:
                wait(pe, latest("bank 2 read"))
                wait(pe, kst_t, it_t)
                for c in range(TT - 1):
                    m = pe.matmul(PS[:, 2, c * P:(c + 1) * P], KST[:, c], ITM[:, c], start=True, stop=True)
                u_mm = PE.mark(m)
                step("kst used", u_mm)
                wait(dve, latest("state used"))
                st = do(DV, [u_mm], dve.tensor_copy, STATE[:, 0], PS[:, 2, 0:P])
                for c in range(1, TT - 1):
                    st = do(DV, [st, qs_t], dve.scalar_tensor_tensor, out=STATE[:, c], in0=STATE[:, c - 1], scalar=DEC[:, c:c + 1],
                            in1=PS[:, 2, c * P:(c + 1) * P], op0=ALU.mult, op1=ALU.add)
                step("bank 2 read", st)
        step("qk used", mm[7])
        run()
        if not last:
            take_qf(marks)
            feed()
        wait(pe, latest("bank 3 read"))
        wait(pe, kept, st, qs_t)
        for c in range(TT):
            cols = slice(c * P, (c + 1) * P)
            m = pe.matmul(PS[:, 3, cols], ITM[:, c], PAIRS[:, c], start=True, stop=c == 0)
            if c:
                m = pe.matmul(PS[:, 3, cols], STATE[:, c - 1], QS[:, cols], start=False, stop=True)
        o_mm = PE.mark(m)
        for name in ("itm", "state", "qs", "pairs"):
            step(name + " used", o_mm)
        wait(act, latest("sqo used"))
        s = do(AC, [o_mm], act.activation, SQO[:, 0], PS[:, 3], ACT.Square)
        o_t = do(DV, [s, gs_t], dve.tensor_tensor, OAR[:, bass.ds(h, 1)].rearrange("p a s -> p (a s)"), PS[:, 3], GS[:, :], ALU.mult)
        step("bank 3 read", o_t)
        step("gs used", o_t)
        wait(dve, latest("ssqo used"))
        ssq = do(DV, [s], dve.tensor_tensor, SSQ[:, :], SSQ[:, :], SQO[:, 0], ALU.add)
        step("sqo used", ssq)
        step("ssqo used", ssq)
        return o_t, ssq

    slot = take()
    run, marks = projection((4, 5), slot)
    run()
    take_qf(marks)
    feed()
    meet()
    with wloop(HG - 1, 2) as i:
        hgrn_head(i, False)
    o_t, ssq = hgrn_head(HG - 1, True)

    def take_qk(marks):
        wait(act, latest("fqk used"))
        t = do(AC, [marks[0]], act.activation, FQ[:, :], PS[:, 4], ACT.Copy)
        step("bank 4 read", t)
        t = do(AC, [marks[1]], act.activation, FK[:, :], PS[:, 5], ACT.Copy)
        step("bank 5 read", t)
        step("fqk ready", t)

    def project_v():
        slot = take()
        mm = linear(6, slot, 0, P, A)
        used(mm)
        feed()
        wait(act, latest("fvf used"))
        t = do(AC, [mm], act.activation, FVF[:, :], PS[:, 6], ACT.Copy)
        step("bank 6 read", t)
        wait(pe, latest("bank 5 read"))
        wait(pe, t)
        for c in range(TT):
            m = pe.transpose(PS[:, 5, c * P:(c + 1) * P], FVF[:, c * P:(c + 1) * P], IDENT[:, :])
        t = PE.mark(m)
        step("fvf used", t)
        wait(act, latest("fv used"))
        t = do(AC, [t], act.activation, FV[:, :, :], PS[:, 5].rearrange("p (c t) -> p c t", t=P), ACT.Copy)
        step("bank 5 read", t)
        step("fv ready", t)

    slot = take()
    run, marks = projection((4, 5), slot)
    run()
    take_qk(marks)
    feed()
    project_v()
    OAH2, OAL2 = sb("OAH2", [P, DB, S], F32R, R + 64), sb("OAL2", [P, DB, S], F32R, R + 80)
    TO = sb("TO", [P, 2, S], F32, R + 110)
    r = root_mean(7, sum_of_blocks(7, [ssq]), D, RIN[:, :])
    oa_t = None
    for d in range(DB):
        wait(dve, latest(f"to{d % 2} used"))
        t = do(DV, [r, o_t], dve.scalar_tensor_tensor, out=TO[:, d % 2], in0=OAR[:, d], scalar=vec("hg_norm_g_2", d, 1),
               in1=RIN[:, :], op0=ALU.mult, op1=ALU.mult)
        oa_t = split_from(TO[:, d % 2], OAH2[:, d], OAL2[:, d], [t])
        step(f"to{d % 2} used", oa_t)
    SMF, PTF = sb("SMF", [P, 1, 10 * P], F32, R + 96), sb("PTF", [P, TT, S], F32, R + 101)
    STATF = sb("STATF", [P, 32], F32, R + 109)
    wait(act, oa_t)
    t = do(DV, [], dve.memset, MASKC[:, :], 0.0)
    for n in (1, 3, 6, 10):
        mask_t = do(DV, [t], dve.tensor_copy, MASKC[:, (n - 1) * P:n * P], CAUSAL[:, :])
    wait(dve, mask_t)

    def fox_head(h, last):
        wait(dve, latest("pickh used"))
        pick_t = do(DV, [], dve.tensor_scalar, PICKH[0:FOX, :], ONES[0:FOX, :], IDENT[0:FOX, bass.ds(h, 1)], None, ALU.mult)
        wait(pe, latest("fqk ready"))
        parts = causal_softmax(SMF, STATF, 0, FQ[:, :], FK[:, :], MASKC, P ** -0.5, (0, 1, 2, 3), [pick_t],
                               key_bias=(PICKH[0:FOX, :], NEGC[0:FOX, :]))
        scored = PE.now()
        step("fqk used", scored)
        step("pickh used", scored)
        if not last:
            slot = take()
            run, marks = projection((4, 5), slot)
            run()
            take_qk(marks)
            feed()
        pt_t = transposed(PTF, parts, (0, 1, 2, 3), 0)
        wait(pe, latest("bank 7 read"), latest("fv ready"))
        o_mm = weighted_values(PTF, PS[:, 7], [FV[:, j] for j in range(TT)], pt_t, None)
        step("fv used", o_mm)
        blk = bass.ds(h, 1)
        hi, lo = (x[:, blk].rearrange("p a s -> p (a s)") for x in (OBH2, OBL2))
        t = do(AC, [o_mm], act.activation, hi, PS[:, 7], ACT.Copy)
        t = do(DV, [t], dve.tensor_tensor, lo, PS[:, 7], hi.bitcast(F32), ALU.subtract)
        step("bank 7 read", t)
        if not last:
            project_v()
        return t, o_mm

    meet()
    with wloop(FOX - 1, 2) as i:
        fox_head(i, False)
    ob_t, o_mm = fox_head(FOX - 1, True)

    ZH2, ZL2 = sb("ZH2", [P, DB, S], F32R, R + 32), sb("ZL2", [P, DB, S], F32R, R + 48)
    SG2, TZ2 = sb("SG2", [P, 2, S], F32, R + 96), sb("TZ2", [P, 2, S], F32, R + 100)
    wait(act, ob_t)
    wait(pe, oa_t, ob_t)
    wait(dve, ob_t, o_mm)
    OA2 = [(OAH2[:, k], OAL2[:, k]) for k in range(DB)]
    OB2 = [(OBH2[:, k], OBL2[:, k]) for k in range(DB)]
    z_t = gated_sum(DB, A, OA2, OB2, 8 * P, SG2, TZ2, ZH2, ZL2, VEC_AT["b_gate_2"])
    Z = [(ZH2[:, k], ZL2[:, k]) for k in range(DB)]
    Y, y_t, ssq = square_linear(Z, [z_t.last()], 88, 98)
    x_t = residual(Y, y_t, ssq, 0, vec("mix_post_g_2"))
    MH, ML = sb("MH", [P, DB, MEM], F32R, R), sb("ML", [P, DB, MEM], F32R, R + 8)
    MEMT = sb("MEMT", [P, DB, MEM], F32, R + 16)
    OMH, OML2 = sb("OMH", [P, DB, S], F32R, R + 32), sb("OML2", [P, DB, S], F32R, R + 48)
    MQ, MK, MV = sb("MQ", [P, 2, S], F32, R + 64), sb("MK", [P, 2, MEM], F32, R + 68), sb("MV", [P, 2, MEM], F32, R + 70)
    SMM, PTM = sb("SMM", [P, TT, MEM], F32, R + 72), sb("PTM", [P, 2, S], F32, R + 76)
    SQM2, TM = sb("SQM2", [P, 2, MEM], F32, R + 80), sb("TM", [P, 2, MEM], F32, R + 82)
    STATM, RINM = sb("STATM", [P, 16], F32, R + 84), sb("RINM", [P, MEM], F32, R + 85)
    s_mem = g.track("memory")
    wait(act, x_t[-1])
    mem_t = s_mem.mark(act.dma_start(MEMT[:, :, :], io["memT"].rearrange("(k p) n -> p k n", p=P)), by=16)
    a_t = prenorm(x_t, vec("mem_pre_g_2"))
    wait(pe, latest("bank 1 read"))
    for d in range(DB):
        wait(act, latest(f"sqm2_{d % 2} used"))
        t = do(AC, [mem_t], act.activation, SQM2[:, d % 2], MEMT[:, d], ACT.Square)
        mm = do(PE, [t], pe.matmul, PS[:, 1, 0:MEM], ONES[:, :], SQM2[:, d % 2], start=d == 0, stop=d == DB - 1)
        step(f"sqm2_{d % 2} used", mm)
    r = root_mean(1, mm, D, RINM[:, :])
    for d in range(DB):
        wait(dve, latest(f"tm{d % 2} used"))
        t = do(DV, [r], dve.scalar_tensor_tensor, out=TM[:, d % 2], in0=MEMT[:, d], scalar=vec("mem_kv_g_2", d, 1),
               in1=RINM[:, :], op0=ALU.mult, op1=ALU.mult)
        m_t = split_from(TM[:, d % 2], MH[:, d], ML[:, d], [t])
        step(f"tm{d % 2} used", m_t)
    MM = [(MH[:, k], ML[:, k]) for k in range(DB)]

    def mem_q():
        slot = take()
        mm = [linear(f, slot, f * P, 2 * P, A) for f in range(2)]
        used(mm[1])
        wait(act, latest("mq used"))
        for f in range(2):
            q_t = do(AC, [mm[f]], act.activation, MQ[:, f], PS[:, f], ACT.Copy)
            step(f"bank {f} read", q_t)
        feed()
        return q_t

    def mem_k():
        slot = take()
        mm = [linear(2 + f, slot, f * P, 2 * P, MM) for f in range(2)]
        used(mm[1])
        wait(act, latest("mk used"))
        for f in range(2):
            k_t = do(AC, [mm[f]], act.activation, MK[:, f], PS[:, 2 + f, 0:MEM], ACT.Copy)
            step(f"bank {2 + f} read", k_t)
        feed()
        return k_t

    def mem_scores(q_t, k_t):
        wait(pe, latest("bank 4 read"), latest("bank 5 read"))
        wait(pe, q_t, k_t)
        for i in range(TT):
            for f in range(2):
                m = pe.matmul(PS[:, 4 + i // 2, (i % 2) * MEM:(i % 2 + 1) * MEM], MQ[:, f, i * P:(i + 1) * P],
                              MK[:, f], start=f == 0, stop=f == 1)
        mm = PE.mark(m)
        step("mq used", mm)
        step("mk used", mm)
        scale = MEM ** -0.5
        banks = PS[:, 4:6].rearrange("p b (i k) -> p (b i) k", k=MEM)
        high, low, sums, inv = (STATM[:, 4 * n:4 * n + 4] for n in range(4))
        wait(dve, latest("smm used"))
        t = do(DV, [mm], dve.tensor_reduce, high, banks, mybir.AxisListType.X, ALU.max)
        t = do(DV, [t], dve.tensor_scalar, low, high, -scale, None, ALU.mult)
        wait(act, latest("smm used"))
        for i in range(TT):
            e = do(AC, [t], act.activation, SMM[:, i], banks[:, i], ACT.Exp, bias=low[:, i:i + 1], scale=scale,
                   accum_out=sums[:, i:i + 1])
        step("bank 4 read", e)
        step("bank 5 read", e)
        t = do(DV, [e], dve.reciprocal, inv, sums)
        for i in range(TT):
            p_t = do(DV, [t], dve.tensor_scalar, SMM[:, i], SMM[:, i], inv[:, i:i + 1], None, ALU.mult)
        return p_t

    def mem_v():
        slot = take()
        for j in range(2):
            wait(pe, latest(f"bank {6 + j} read"))
            n = 0
            for k in range(DB):
                for wt, x in ((WHI, MH), (WHI, ML), (WLO, MH)):
                    m = pe.matmul(PS[:, 6 + j, 0:MEM], x[:, k, j * P:(j + 1) * P], wt[:, slot, k * MEM:(k + 1) * MEM],
                                  start=n == 0, stop=n == 3 * DB - 1)
                    n += 1
            mm = PE.mark(m)
            wait(act, latest("mv used"))
            v_t = do(AC, [mm], act.activation, MV[:, j], PS[:, 6 + j, 0:MEM], ACT.Copy)
            step(f"bank {6 + j} read", v_t)
        used(mm)
        feed()
        return v_t

    def mem_values(block, p_t, v_t):
        for j in range(2):
            wait(pe, latest(f"bank {4 + j} read"))
        wait(pe, p_t)
        wait(act, latest("ptm used"))
        for j in range(2):
            for i in range(TT):
                m = pe.transpose(PS[:, 4 + j, i * P:(i + 1) * P], SMM[:, i, j * P:(j + 1) * P], IDENT[:, :])
            m = PE.mark(m)
            pt_t = do(AC, [m], act.activation, PTM[:, j], PS[:, 4 + j], ACT.Copy)
            step(f"bank {4 + j} read", pt_t)
        step("smm used", m)
        wait(pe, pt_t, v_t)
        for f in range(2):
            wait(pe, latest(f"bank {6 + f} read"))
            for j in range(2):
                m = pe.matmul(PS[:, 6 + f], MV[:, j, f * P:(f + 1) * P], PTM[:, j], start=j == 0, stop=j == 1)
            m = PE.mark(m)
            hi, lo = (x[:, bass.ds(block + f, 1)].rearrange("p a s -> p (a s)") for x in (OMH, OML2))
            t = do(AC, [m], act.activation, hi, PS[:, 6 + f], ACT.Copy)
            t = do(DV, [t], dve.tensor_tensor, lo, PS[:, 6 + f], hi.bitcast(F32), ALU.subtract)
            step(f"bank {6 + f} read", t)
        step("ptm used", m)
        step("mv used", m)
        return t

    wait(pe, *a_t, m_t)
    meet()
    with wloop(MEM_H // 2, 6) as i:
        q_t, k_t = mem_q(), mem_k()
        p_t = mem_scores(q_t, k_t)
        v_t = mem_v()
        q_t = mem_q()
        mem_values(i * 4, p_t, v_t)
        k_t = mem_k()
        p_t = mem_scores(q_t, k_t)
        v_t = mem_v()
        om_t = mem_values(i * 4 + 2, p_t, v_t)
    OM = [(OMH[:, k], OML2[:, k]) for k in range(DB)]
    Y, y_t, ssq = square_linear(OM, [om_t.last()], 88, 98)
    x_t = residual(Y, y_t, ssq, 0, vec("mem_post_g_2"))
    a_t = prenorm(x_t, vec("ffn2_pre_g_2"))
    x_t = ffn(a_t, coef(7))

    while stream["fed"] < n_chunks:
        feed()

    s_out = nc.alloc_semaphore("s_out")
    for d in range(DB):
        wait(act, x_t[d])
        act.dma_start(io["out"][d * P:(d + 1) * P, :], X[:, d]).then_inc(s_out, 16)
    act.wait_ge(s_out, DB * 16)
    n_taken.append((stream["taken"], stream["fed"]))
    return g.counted


n_taken = []


def weight_chunks(w):
    out = []

    def blocks(a, rows=P):
        return a.reshape(-1, P, a.shape[1]).transpose(1, 0, 2).reshape(P, -1)

    def chunk(*parts):
        a = np.concatenate(parts, 1)
        out.append(np.pad(a, ((0, 0), (0, CH - a.shape[1]))))

    def ffn(gate, up, down):
        for i in range(FB // 2):
            chunk(blocks(gate[:, i * 256:(i + 1) * 256]))
            chunk(blocks(up[:, i * 256:(i + 1) * 256]))
        for c in range(FB // 2):
            chunk(blocks(down[c * 256:(c + 1) * 256]))

    def square(a):
        for i in range(a.shape[1] // 256):
            chunk(blocks(a[:, i * 256:(i + 1) * 256]))

    w1 = {k: v[0] for k, v in w.items()}
    ffn(w1["w_gate1"], w1["w_up1"], w1["w_down1"])
    w_in = np.concatenate([w1["w_in"][:, :712], np.zeros((D, 56), np.float32)], 1)
    for i in range(3):
        chunk(blocks(w_in[:, i * 256:(i + 1) * 256]))
    chunk(blocks(w1["w_iq"].reshape(Q_LORA, -1)))
    square(w1["w_in"][:, 712:3016])
    for i in range(4):
        hs = slice(2 * i, 2 * i + 2)
        chunk(blocks(w1["w_uq"][:, hs].reshape(Q_LORA, -1)), blocks(w1["w_uk"][:, hs].reshape(KV_LORA, -1)),
              blocks(w1["w_uv"][:, hs].reshape(KV_LORA, -1)))
    for d in range(DB):
        c = slice(d * P, (d + 1) * P)
        chunk(blocks(w1["w_in"][:, 3016:4040][:, c]), blocks(w1["w_in"][:, 4040:5064][:, c]))
        chunk(blocks(w1["w_up_a"][:, c]), blocks(w1["w_up_b"][:, c]))
    square(w1["w_o"])
    ffn(w1["w_gate2"], w1["w_up2"], w1["w_down2"])
    w2 = {k[:-2]: v[0] for k, v in w.items() if k.endswith("_2") and v.ndim == 3}
    ffn(w2["ffn1_w_in"][:, :FF], w2["ffn1_w_in"][:, FF:], w2["ffn1_w_down"])
    q_a, f_a, i_a, g_a, q_b, k_b, v_b = (w2["w_in"][:, n * D:(n + 1) * D] for n in range(7))
    f_b, gates = w2["w_in"][:, 7 * D:7 * D + FOX], w2["w_in"][:, 7 * D + FOX:]
    chunk(blocks(np.pad(f_b, ((0, 0), (0, P - FOX)))))

    def pair(a, b, h):
        c = slice(h * P, (h + 1) * P)
        chunk(blocks(np.concatenate([a[:, c], b[:, c]], 1)))

    pair(q_a, f_a, 0)
    for h in range(HG):
        pair(i_a, g_a, h)
        if h < HG - 1:
            pair(q_a, f_a, h + 1)
    pair(q_b, k_b, 0)
    for h in range(FOX):
        chunk(blocks(v_b[:, h * P:(h + 1) * P]))
        if h < FOX - 1:
            pair(q_b, k_b, h + 1)
    for d in range(DB):
        c = slice(d * P, (d + 1) * P)
        chunk(blocks(gates[:, :D][:, c]), blocks(gates[:, D:][:, c]))
        chunk(blocks(w2["w_branch_a"][:, c]), blocks(w2["w_branch_b"][:, c]))
    square(w2["w_out"])
    for h in range(MEM_H):
        c = slice(h * MEM, (h + 1) * MEM)
        for a in (w2["w_mq"], w2["w_mkv"][:, :D], w2["w_mkv"][:, D:]):
            chunk(blocks(a[:, c]))
    square(w2["w_mo"])
    ffn(w2["ffn2_w_in"][:, :FF], w2["ffn2_w_in"][:, FF:], w2["ffn2_w_down"])
    if len(out) % 2:
        out.append(out[-1])
    return np.stack(out)


_STAGE = "end"


def kernel(**inputs):
    import concourse.bacc as _bacc
    from concourse.bass_utils import run_bass_kernel_spmd as _run

    w = {k: np.asarray(v) for k, v in inputs.items()}
    mod_w = w["w_mod"][0].reshape(DB, P, NMOD, P).transpose(1, 2, 0, 3).reshape(P, NMOD, D)
    arrays = {
        "xT": np.ascontiguousarray(w["x"][0].T),
        "memT": np.ascontiguousarray(w["mem_2"][0].T),
        "positions": np.ascontiguousarray(w["positions"]),
        "fox_bias": np.ascontiguousarray(w["fox_f_bias_2"].reshape(FOX, 1)),
        "vecs": np.ascontiguousarray(np.concatenate([w[n].reshape(-1, P) for n, _ in VECS]).T),
        "w_mod": np.ascontiguousarray(np.pad(mod_w, ((0, 0), (0, MBLK), (0, 0)))),
        "weights": weight_chunks(w),
        "consts": CONSTS,
    }
    counts = {}
    for _ in range(2):
        nc = _bacc.Bacc("TRN2", target_bir_lowering=False, num_devices=1, dynamic_dma_scratch_size=256)
        io = {n: nc.dram_tensor(f"in_{n}", a.shape, mybir.dt.from_np(a.dtype), kind="ExternalInput").ap()
              for n, a in arrays.items()}
        io["out"] = nc.dram_tensor("out_xT", (D, S), F32, kind="ExternalOutput").ap()
        counts = build(nc, io, counts, _STAGE)
    r = _run(nc, [{f"in_{n}": a for n, a in arrays.items()}], core_ids=[0])
    return np.ascontiguousarray(r.results[0]["out_xT"].T)[None]
```

```python
import math
from contextlib import contextmanager

import concourse.bass as bass
import numpy as np
from concourse import mybir

F32 = mybir.dt.float32
F32R = mybir.dt.float32r
I32 = mybir.dt.int32
U8 = mybir.dt.uint8
ALU = mybir.AluOpType
ACT = mybir.ActivationFunctionType
ENG = mybir.EngineType

P = 128
S = 512
D = 1024
FF = 2816
DB = D // P
FB = FF // P
TT = S // P
CH = 2048
NMOD = 9 * DB
MBLK = 5
M_FIRST = NMOD - (FB // 2) * MBLK
EPS = 1e-6
NEG = -1e30

NOPE, ROPE_A, D_QK, Q_LORA, KV_LORA, TOPK = 64, 32, 96, 384, 256, 128
H_A, H_IDX, H_B, HG, FOX, MEM_H, MEM = 8, 8, 4, 8, 8, 4, 256


class Ticket:

    def __init__(self, track, value, k=0, loop=None):
        self.track, self.value, self.k, self.loop = track, value, k, loop

    def last(self, back=0):
        if self.loop is None or not self.loop.closed:
            return self
        start, stride = self.loop.start[self.track], self.loop.stride[self.track]
        return Ticket(self.track, start + (self.loop.n - 1 - back) * stride + self.k)


class Track:

    def __init__(self, nc, name, eng=None, head_start=0):
        self.name, self.eng, self.sem = name, eng, nc.alloc_semaphore("s_" + name)
        self.base, self.k, self.stride, self.loop = 0, 0, 0, None
        if head_start:
            eng.sem_inc(self.sem, head_start)
            self.base = head_start

    def mark(self, ins, by=1):
        ins.then_inc(self.sem, by)
        self.k += by
        return self.now()

    def now(self):
        return Ticket(self, self.base + self.k, self.k, self.loop)


class Loop:

    def __init__(self, n):
        self.n, self.start, self.stride, self.closed = n, {}, {}, False


class Counting:

    def __init__(self, nc, before):
        self.nc, self.before, self.counted = nc, before, {}
        self.tracks, self.steps, self.inside, self.seen, self.number = {}, {}, None, {}, 0

    def track(self, name, eng=None, head_start=0):
        self.tracks[name] = Track(self.nc, name, eng, head_start)
        return self.tracks[name]

    def next_name(self):
        self.number += 1
        return self.number

    def wait(self, eng, *tickets):
        for t in tickets:
            if t is None:
                continue
            t = t.last()
            if isinstance(t.value, int):
                key = (str(eng.engine), t.track.name)
                if t.value <= self.seen.get(key, 0):
                    continue
                self.seen[key] = t.value
            eng.wait_ge(t.track.sem, t.value)

    def step(self, name, ticket):
        self.steps[name] = ticket

    def latest(self, name):
        t, lp = self.steps.get(name), self.inside
        if lp is not None and (t is None or t.loop is not lp[0]) and name in lp[1]:
            track, k = lp[1][name]
            track = self.tracks[track]
            return Ticket(track, track.base + (k - track.stride))
        return t

    def meet(self):
        tickets = [Ticket(t, t.base + t.k) for t in self.tracks.values() if t.eng is not None]
        for ticket in tickets:
            self.wait(ticket.track.eng, *tickets)

    @contextmanager
    def loop(self, n):
        key = len(self.counted)
        self.counted[key] = None
        known = self.before.get(key, {"stride": {}, "steps": {}})
        lp, seen = Loop(n), dict(self.seen)
        with self.nc.Fori(0, n, engines=[ENG.PE, ENG.Activation, ENG.DVE]) as i:
            for name, t in self.tracks.items():
                lp.start[t] = t.base + t.k
                lp.stride[t] = t.stride = known["stride"].get(name, 0)
                t.base = i * t.stride + lp.start[t] if t.stride else lp.start[t]
                t.k, t.loop = 0, lp
            self.inside = (lp, known["steps"])
            yield i
        self.inside = None
        self.counted[key] = {"stride": {name: t.k for name, t in self.tracks.items()},
                             "steps": {name: (t.track.name, t.k) for name, t in self.steps.items() if t.loop is lp}}
        assert key not in self.before or known == self.counted[key], "the two builds differ"
        for t in self.tracks.values():
            lp.stride[t] = t.k
            t.base, t.k, t.stride, t.loop = lp.start[t] + n * t.k, 0, 0, None
        lp.closed = True
        self.seen = seen




VECS = [("c", DB), ("b_mod", NMOD), ("g_pre_ffn1", DB), ("g_post_ffn1", DB), ("g_pre_mix", DB),
        ("g_cq", Q_LORA // P), ("g_ckv", KV_LORA // P), ("g_post_mix", DB), ("g_pre_ffn2", DB),
        ("g_post_ffn2", DB), ("ffn1_pre_g_2", DB), ("ffn1_post_g_2", DB), ("mix_pre_g_2", DB),
        ("hg_norm_g_2", DB), ("b_gate_2", 2 * DB), ("mix_post_g_2", DB), ("mem_pre_g_2", DB),
        ("mem_kv_g_2", DB), ("mem_post_g_2", DB), ("ffn2_pre_g_2", DB), ("ffn2_post_g_2", DB),
        ("hg_lb_logits_2", 2 * DB)]
VEC_AT = {name: sum(n for _, n in VECS[:i]) for i, (name, _) in enumerate(VECS)}
NVEC = sum(n for _, n in VECS)


def constants():
    i = np.arange(P)
    q, k = i[:, None], i[None, :]
    c = {"ident": (q == k) * 1.0, "causal": np.where(k <= q, 0.0, NEG)}
    for m in range(7):
        d = 4 * (q - k) - (m - 3)
        c[f"near{m}"] = np.where((d >= 0) & (d <= 128), 0.0, NEG)
    c["far1"] = c["causal"]
    c["far2"] = np.where((q >= k) & ((q - k) % 4 == 0), 0.0, NEG)

    def rotation(half, start=0, stop=P):
        r = np.zeros((P, P))
        for p in range(start, stop):
            first = p % (2 * half) < half
            r[p, p + half if first else p - half] = -1.0 if first else 1.0
        return r

    pick_ki, pick_kr = np.zeros((P, P)), np.zeros((P, P))
    pick_ki[i, 32 + i % 32] = 1.0
    pick_kr[NOPE + i[:ROPE_A], i[:ROPE_A]] = 1.0
    rot_q = rotation(16, NOPE, D_QK)
    for name, m in (("rot32", rotation(16)), ("rot64", rotation(32)), ("rot_q", rot_q),
                    ("pick_ki", pick_ki), ("rot_ki", rotation(16) @ pick_ki),
                    ("pick_kr", pick_kr), ("rot_kr", rot_q @ pick_kr)):
        c[name] = m.T
    f32 = np.float32
    inv16 = f32(10000.0) ** (-np.arange(16, dtype=f32) / f32(16))
    inv32 = f32(10000.0) ** (-np.arange(32, dtype=f32) / f32(32))
    c["inv"] = np.stack([inv16[i % 16], inv32[i % 32]], 1)
    c["reset"] = np.ones((P, 1)) * (np.arange(S) % P != 0)
    lev = np.zeros((P, 8, P))
    lev[:, 0] = q == k
    for j in range(7):
        w = 2 << j
        lev[:, j + 1] = (q // w == k // w) & (q % w < w // 2) & (k % w >= w // 2)
    c["levels"] = lev.reshape(P, 8 * P)
    at, n = {}, 0
    for name, a in c.items():
        at[name] = n
        n += a.shape[1]
    return np.concatenate([a.astype(f32) for a in c.values()], 1), at


CONSTS, CONST_AT = constants()


def build(nc, io, counts, upto):
    g = Counting(nc, counts)
    wait, step, latest, meet = g.wait, g.step, g.latest, g.meet
    pe, act, dve, pool, sp = nc.tensor, nc.scalar, nc.vector, nc.gpsimd, nc.sync
    PE, AC, DV = (g.track(n, e, 512) for n, e in (("pe", pe), ("act", act), ("dve", dve)))

    def do(track, waits, fn, *args, **kw):
        wait(track.eng, *waits)
        return track.mark(fn(*args, **kw))

    def sb(name, shape, dt, kb):
        return nc.alloc_sbuf_tensor_at(name, shape, dt, offset=512 + int(round(kb * 1024)))

    X = sb("X", [P, DB, S], F32, 0)
    RAW = sb("RAW", [P, 2, CH], F32, 16)
    WHI = sb("WHI", [P, 2, CH], F32R, 32)
    WLO = sb("WLO", [P, 2, CH], F32R, 48)
    AHI = sb("AHI", [P, DB, S], F32R, 64)
    ALO = sb("ALO", [P, DB, S], F32R, 80)
    ONES = sb("ONES", [P, P], F32, 96)
    IDENT = sb("IDENT", [P, P], F32, 96.5)
    CAUSAL = sb("CAUSAL", [P, P], F32, 97)
    VEC = sb("VEC", [P, NVEC], F32, 97.5)
    MOD = sb("MOD", [P, NMOD], F32, 98.75)
    COEF = sb("COEF", [P, 16 * DB], F32, 99.125)
    CCOL = sb("CCOL", [P, DB], F32, 99.6875)
    EPSC = sb("EPSC", [P, 1], F32, 99.75)
    RIN = sb("RIN", [P, S], F32, 100)
    SSQ = sb("SSQ", [P, S], F32, 102)
    R = 104
    PS = nc.alloc_psum_tensor("PS", [P, 8, S], F32)

    def vec(name, d=0, n=DB):
        return VEC[:, VEC_AT[name] + d:VEC_AT[name] + d + n]

    n_chunks = io["weights"].shape[0]
    loaded = [nc.alloc_semaphore("s_loaded0"), nc.alloc_semaphore("s_loaded1")]
    s_high, s_low = nc.alloc_semaphore("s_high"), nc.alloc_semaphore("s_low")
    stream = {"fed": 0, "taken": 0, "free": [], "per": 0, "i": None}

    def start_stream():
        for j in range(2):
            sp.dma_start(RAW[:, j], io["weights"][j]).then_inc(loaded[j], 16)
        with sp.Fori(1, n_chunks // 2) as i:
            for j in range(2):
                sp.wait_ge(s_low, i * 2 + (j - 1))
                sp.dma_start(RAW[:, j], io["weights"][bass.ds(i * 2 + j, 1)].rearrange("a p c -> (a p) c")) \
                    .then_inc(loaded[j], 16)
        with pool.Fori(0, n_chunks // 2) as i:
            for j in range(2):
                pool.wait_ge(s_high, i * 2 + (j + 1))
                pool.tensor_tensor(WLO[:, j], RAW[:, j], WHI[:, j].bitcast(F32), ALU.subtract) \
                    .then_inc(s_low, 1)

    def feed():
        if stream["i"] is None and stream["fed"] == n_chunks:
            return
        slot, turn = stream["fed"] % 2, stream["fed"] // 2 + 1
        if stream["i"] is not None:
            turn = stream["i"] * (stream["per"] // 2) + turn
        if stream["free"]:
            wait(act, stream["free"].pop(0))
        act.wait_ge(loaded[slot], turn * 16)
        act.activation(WHI[:, slot], RAW[:, slot], ACT.Copy).then_inc(s_high, 1)
        stream["fed"] += 1

    def take():
        n = stream["taken"] + 1
        if stream["i"] is not None:
            n = stream["i"] * stream["per"] + n
        pe.wait_ge(s_low, n)
        stream["taken"] += 1
        return (stream["taken"] - 1) % 2

    def used(ticket):
        stream["free"].append(ticket)

    @contextmanager
    def wloop(n, per):
        with g.loop(n) as i:
            stream["i"], stream["per"] = i, per
            fed, taken = stream["fed"], stream["taken"]
            yield i
            assert stream["fed"] == fed + per and stream["taken"] == taken + per and per % 2 == 0
            stream["i"], stream["per"] = None, 0
        stream["fed"], stream["taken"] = fed + n * per, taken + n * per

    def products(out, slot, pairs, first=True, last=True, ready=()):
        n, m = len(pairs), None
        for q, (cols, (hi, lo)) in enumerate(pairs):
            wait(pe, *ready[q:q + 1])
            for r, (wt, x) in enumerate(((WHI, hi), (WHI, lo), (WLO, hi))):
                m = pe.matmul(out, wt[:, slot, cols], x, start=first and q == 0 and r == 0,
                              stop=last and q == n - 1 and r == 2)
        return m

    def linear(bank, slot, at, step, rhs, width=P, rows=P, ready=()):
        wait(pe, latest(f"bank {bank} read"))
        n = rhs[0][0].shape[-1]
        m = products(PS[0:rows, bank, 0:n], slot,
                     [(slice(at + q * step, at + q * step + width), x) for q, x in enumerate(rhs)], ready=ready)
        return PE.mark(m)

    def two_blocks(banks, slot, rhs, ready):
        m = {}
        wait(pe, *[latest(f"bank {bank} read") for bank in banks])
        for q, x in enumerate(rhs):
            wait(pe, ready[q])
            for f, bank in enumerate(banks):
                at = q * 2 * P + f * P
                m[f] = products(PS[:, bank], slot, [(slice(at, at + P), x)], first=q == 0, last=q == len(rhs) - 1)
                if q == len(rhs) - 1:
                    m[f] = PE.mark(m[f])
        return [m[0], m[1]]

    A = [(AHI[:, k], ALO[:, k]) for k in range(DB)]

    def split_from(src, hi, lo, waits, bias=None):
        if bias is None:
            t1 = do(AC, waits, act.activation, hi, src, ACT.Copy)
            t2 = do(DV, [t1], dve.tensor_tensor, lo, src, hi.bitcast(F32), ALU.subtract)
        else:
            t1 = do(AC, waits, act.activation, hi, src, ACT.Identity, bias=bias)
            t2 = do(DV, [t1], dve.scalar_tensor_tensor, out=lo, in0=src, scalar=bias,
                    in1=hi.bitcast(F32), op0=ALU.add, op1=ALU.subtract)
        return t2

    def tables(name):
        act.preload_act_table_set(name + "_and_others")

    def root_mean(bank, sums_t, n, out, rows=P):
        t = do(AC, [sums_t], act.activation, out, PS[:, bank, 0:out.shape[-1]], ACT.Ln, bias=EPSC[:, 0:1],
               scale=1.0 / n)
        step(f"bank {bank} read", t)
        return do(AC, [t], act.activation, out, out, ACT.Exp, scale=-0.5)

    def prenorm(x_t, mul, shift=None):
        SQ = sb(f"SQ{g.next_name()}", [P, 2, S], F32, R + 88)
        T = sb(f"T{g.next_name()}", [P, 3, S], F32, R + 92)
        sq_t, mm_t = [], []
        wait(act, x_t[0])
        wait(dve, x_t[-1])
        tables("natural_log_exp")
        wait(pe, latest("bank 0 read"))
        for d in range(DB):
            sq_t.append(do(AC, [x_t[d], mm_t[d - 2] if d > 1 else None], act.activation,
                           SQ[:, d % 2], X[:, d], ACT.Square))
            mm_t.append(do(PE, [sq_t[d]], pe.matmul, PS[:, 0], ONES[:, :], SQ[:, d % 2],
                           start=d == 0, stop=d == DB - 1))
        r = root_mean(0, mm_t[-1], D, RIN[:, :])
        wait(act, *mm_t[-1:])
        a_t, high_t = [], []
        for d in range(DB + 1):
            if d < DB:
                t = do(DV, [r, a_t[d - 3] if d > 2 else None], dve.scalar_tensor_tensor, out=T[:, d % 3], in0=X[:, d],
                       scalar=mul[:, d:d + 1], in1=RIN[:, :], op0=ALU.mult, op1=ALU.mult)
                high_t.append(do(AC, [t], act.activation, AHI[:, d], T[:, d % 3], ACT.Identity,
                                 bias=0.0 if shift is None else shift[:, d:d + 1]))
            if d > 0:
                e = d - 1
                a_t.append(do(DV, [high_t[e]], dve.scalar_tensor_tensor, out=ALO[:, e], in0=T[:, e % 3],
                              scalar=0.0 if shift is None else shift[:, e:e + 1],
                              in1=AHI[:, e].bitcast(F32), op0=ALU.add, op1=ALU.subtract))
        return a_t

    def sum_of_blocks(bank, waits):
        wait(pe, latest(f"bank {bank} read"))
        return do(PE, waits, pe.matmul, PS[:, bank], ONES[:, :], SSQ[:, :], start=True, stop=True)

    def residual(Y, y_t, bank, coef):
        T = sb(f"T{g.next_name()}", [P, 3, S], F32, R + 92)
        r = root_mean(bank, sum_of_blocks(bank, [latest("squares added")]), D, RIN[:, :])
        feed()
        x_t, t = [], [None] * DB
        for d in range(DB + 1):
            if d < DB:
                t[d] = do(DV, [r, y_t[d], x_t[d - 3] if d > 2 else None], dve.scalar_tensor_tensor,
                          out=T[:, d % 3], in0=Y[:, d],
                          scalar=coef[:, d:d + 1], in1=RIN[:, :], op0=ALU.mult, op1=ALU.mult)
            if d > 0:
                x_t.append(do(DV, [t[d - 1]], dve.tensor_tensor, X[:, d - 1], X[:, d - 1],
                              T[:, (d - 1) % 3], ALU.add))
        return x_t

    def take_output(Y, SQ, bank, d, mm_t, outs):
        wait(act, latest(f"sq{d % 2} used"))
        y = do(AC, [mm_t], act.activation, Y[:, d], PS[:, bank], ACT.Copy)
        step(f"bank {bank} read", y)
        outs.append((d, y, do(AC, [y], act.activation, SQ[:, d % 2], Y[:, d], ACT.Square)))
        if len(outs) == 1:
            t = do(DV, [outs[0][2]], dve.tensor_copy, SSQ[:, :], SQ[:, d % 2])
        else:
            t = do(DV, [outs[-1][2], latest("squares added")], dve.tensor_tensor, SSQ[:, :], SSQ[:, :], SQ[:, d % 2], ALU.add)
        step(f"sq{d % 2} used", t)
        step("squares added", t)

    def ffn(a_t, coef, between=None, late=None):
        u = g.next_name()
        HHI = sb(f"HHI{u}", [P, FB, S], F32R, R)
        HLO = sb(f"HLO{u}", [P, FB, S], F32R, R + 44)
        SIL = sb(f"SIL{u}", [P, 2, S], F32, R + 88)
        PRD = sb(f"PRD{u}", [P, 2, S], F32, R + 92)
        Y = sb(f"Y{u}", [P, DB, S], F32, R + 98)
        tables("silu")
        with wloop(FB // 2, 2) as i:
            if between:
                between[0](i)
            slot = take()
            gate_t = two_blocks((0, 1), slot, A, a_t)
            used(gate_t[1])
            sil_t = []
            for f in range(2):
                wait(act, latest(f"sil{f} used"))
                sil_t.append(do(AC, [gate_t[f]], act.activation, SIL[:, f], PS[:, f], ACT.Silu))
                step(f"bank {f} read", sil_t[f])
            feed()
            if between:
                between[1](i)
                between[2](i)
            slot = take()
            up_t = [linear(2 + f, slot, f * P, 2 * P, A) for f in range(2)]
            used(up_t[1])
            prd_t, hi_t = [], []
            for f in range(2):
                wait(dve, latest(f"prd{f} used"))
                prd_t.append(do(DV, [up_t[f], sil_t[f]], dve.tensor_tensor, PRD[:, f], PS[:, 2 + f],
                                SIL[:, f], ALU.mult))
                step(f"bank {2 + f} read", prd_t[f])
                step(f"sil{f} used", prd_t[f])
                hi_t.append(do(AC, [prd_t[f]], act.activation, HHI[:, bass.ds(i * 2 + f, 1)],
                               PRD[:, f:f + 1], ACT.Copy))
            for f in range(2):
                h_t = do(DV, [hi_t[f]], dve.tensor_tensor, HLO[:, bass.ds(i * 2 + f, 1)], PRD[:, f:f + 1],
                         HHI[:, bass.ds(i * 2 + f, 1)].bitcast(F32), ALU.subtract)
                step(f"prd{f} used", h_t)
            feed()
        order = [4, 5, 6, 7, 0, 1, 2, 3]

        def down(blocks, first=False, last=False):
            slot = take()
            for d in order:
                if first:
                    wait(pe, latest(f"bank {d} read"))
                m = products(PS[:, d], slot, [(slice(k * D + d * P, k * D + (d + 1) * P), x)
                                              for k, x in enumerate(blocks)], first=first, last=last)
                if last:
                    y_mm[d] = PE.mark(m)
            if last:
                return slot
            used(PE.mark(m))
            feed()

        y_mm = {}
        wait(pe, h_t.last(back=1))
        down([(HHI[:, k], HLO[:, k]) for k in range(2)], first=True)
        wait(pe, h_t)
        with wloop(FB // 4 - 1, 2) as i:
            for j in range(2):
                down([(HHI[:, bass.ds(i * 4 + (2 * j + 2 + k), 1)].rearrange("p a s -> p (a s)"),
                       HLO[:, bass.ds(i * 4 + (2 * j + 2 + k), 1)].rearrange("p a s -> p (a s)"))
                      for k in range(2)])
        down([(HHI[:, k], HLO[:, k]) for k in (FB - 4, FB - 3)])
        down([(HHI[:, k], HLO[:, k]) for k in (FB - 2, FB - 1)], last=True)
        outs = []
        wait(act, h_t)
        tables("natural_log_exp")
        if late:
            late()
        if between:
            act.wait_ge(s_mw[1].sem, first_mw + 16 * (FB // 2))
        for d in order:
            take_output(Y, SIL, d, d, y_mm[d], outs)
        used(y_mm[order[-1]])
        return residual(Y, {d: y for d, y, _ in outs}, order[0], coef)

    s_in, s_x, s_id = g.track("in"), g.track("x"), g.track("id")
    t_vec = s_in.mark(sp.dma_start(VEC[:, :], io["vecs"]), by=16)
    MW = [sb("MW0", [P, MBLK, D], F32, R), sb("MW1", [P, MBLK, D], F32, R + 99)]
    s_mw = [g.track("mw0"), g.track("mw1")]
    groups = [(b, min(MBLK, M_FIRST - b)) for b in range(0, M_FIRST, MBLK)]
    which = [(len(groups) - 1 - n) % 2 for n in range(len(groups))]
    mw_t = []
    eps_t = do(DV, [], dve.memset, EPSC[:, :], EPS)
    ones_t = do(DV, [], dve.memset, ONES[:, :], 1.0)
    wait(pe, ones_t)
    silu_c = do(AC, [t_vec], act.activation, CCOL[:, :], vec("c"), ACT.Silu)

    def weigh_rows(waits, which, nb):
        wait(dve, silu_c, *waits)
        part = [MW[which][:, 0:nb, k * P:(k + 1) * P] for k in range(DB)]
        t = [None, None]
        for k in range(DB):
            if k < 2:
                t[k] = do(DV, [], dve.tensor_scalar, part[k], part[k], CCOL[:, k:k + 1], None, ALU.mult)
            else:
                t[k % 2] = do(DV, [t[k % 2]], dve.scalar_tensor_tensor, out=part[k % 2], in0=part[k],
                              scalar=CCOL[:, k:k + 1], in1=part[k % 2], op0=ALU.mult, op1=ALU.add)
        return t

    def mod_columns(t, which, b0, nb):
        wait(pe, latest("bank 4 read"))
        wait(pe, *t)
        for b in range(nb):
            for k in range(2):
                m = pe.matmul(PS[:, 4, b:b + 1], MW[which][:, b, k * P:(k + 1) * P], ONES[:, 0:1],
                              start=k == 0, stop=k == 1)
        mm = PE.mark(m)
        off = VEC_AT["b_mod"]
        at, vat = (slice(b0, b0 + nb), slice(off + b0, off + b0 + nb)) if isinstance(b0, int) \
            else (bass.ds(b0, nb), bass.ds(b0 + off, nb))
        t = do(DV, [mm, t_vec], dve.tensor_tensor, MOD[:, at], PS[:, 4, 0:nb], VEC[:, vat], ALU.add)
        step("bank 4 read", t)
        step(f"mw{which} used", mm)
        return t

    for n, (b0, nb) in enumerate(groups):
        if n == 2:
            x_in = s_x.mark(sp.dma_start(X[:, :, :], io["xT"].rearrange("(k p) n -> p k n", p=P)), by=16)
            t_id = s_id.mark(sp.dma_start(IDENT[:, :], io["consts"][:, CONST_AT["ident"]:CONST_AT["ident"] + P]), by=16)
            t_id = s_id.mark(sp.dma_start(CAUSAL[:, :], io["consts"][:, CONST_AT["causal"]:CONST_AT["causal"] + P]), by=16)
        if n >= 2:
            wait(sp, latest(f"mw{which[n]} used"))
        mw_t.append(s_mw[which[n]].mark(sp.dma_start(MW[which[n]][:, 0:nb], io["w_mod"][:, b0:b0 + nb]), by=16))
        mod_t = mod_columns(weigh_rows([mw_t[n]], which[n], nb), which[n], b0, nb)
    start_stream()
    wait(act, t_id)
    wait(dve, t_id)
    wait(act, latest("mw1 used"))
    mw_t = s_mw[1].mark(act.dma_start(MW[1][:, 0:MBLK], io["w_mod"][:, M_FIRST:M_FIRST + MBLK]), by=16)
    first_mw = mw_t.value
    feed()
    feed()

    def coef(n):
        return COEF[:, n * DB:(n + 1) * DB]

    def mod(n):
        return MOD[:, n * DB:(n + 1) * DB]

    def scaled(n, gain, m):
        return do(DV, [mod_t, t_vec], dve.scalar_tensor_tensor, out=coef(n), in0=mod(m), scalar=1.0,
                  in1=vec(gain), op0=ALU.add, op1=ALU.mult)

    def gated(n, gain, m, by):
        return do(DV, [mod_t, t_vec], dve.scalar_tensor_tensor, out=coef(n), in0=mod(m), scalar=by,
                  in1=vec(gain), op0=ALU.mult, op1=ALU.mult)

    c0 = scaled(0, "g_pre_ffn1", 1)
    wait(dve, c0, eps_t, ones_t)
    wait(act, eps_t)
    wait(pe, ones_t)
    a_t = prenorm([x_in] * DB, coef(0), mod(0))

    weighed = []

    def mod_weigh(i):
        dve.wait_ge(s_mw[1].sem, i * 16 + first_mw)
        weighed[:] = weigh_rows([], 1, MBLK)

    def mod_sum(i):
        nonlocal mod_t
        mod_t = mod_columns(weighed, 1, i * MBLK + M_FIRST, MBLK)

    def mod_load(i):
        wait(act, latest("mw1 used"))
        act.dma_start(MW[1][:, 0:MBLK], io["w_mod"][:, bass.ds(i * MBLK + (M_FIRST + MBLK), MBLK)]) \
            .then_inc(s_mw[1].sem, 16)

    def all_coefficients():
        gated(1, "g_post_ffn1", 2, 0.5)
        scaled(2, "g_pre_mix", 4)
        gated(3, "g_post_mix", 5, 1.0)
        scaled(4, "g_pre_ffn2", 7)
        gated(5, "g_post_ffn2", 8, 0.5)
        for n, gain in ((6, "ffn1_post_g_2"), (7, "ffn2_post_g_2")):
            t = do(DV, [], dve.tensor_scalar, coef(n), vec(gain), 0.5, None, ALU.mult)
        wait(dve, t)

    x_t = ffn(a_t, coef(1), between=(mod_weigh, mod_sum, mod_load), late=all_coefficients)
    a_t = prenorm(x_t, coef(2), mod(3))

    def const_into(dst, name, sem):
        c = CONST_AT[name]
        return sem.mark(act.dma_start(dst, io["consts"][:, c:c + dst.shape[-1]]), by=16)

    CQH, CQL = (sb(n, [P, 3, S], F32R, R + at) for n, at in (("CQH", 0), ("CQL", 6)))
    CKH, CKL = (sb(n, [P, 2, S], F32R, R + at) for n, at in (("CKH", 12), ("CKL", 16)))
    QKB = sb("QKB", [P, 12, S], F32, R + 20)
    VB = sb("VB", [P, 4, 768], F32, R + 44)
    COSQ, SINQ = sb("COSQ", [P, S], F32, R + 56), sb("SINQ", [P, S], F32, R + 58)
    SEL = sb("SEL", [P, 10 * P], F32, R + 60)
    ROTQ = sb("ROTQ", [P, P], F32, R + 65)
    INV = sb("INV", [P, 2], F32, R + 65.5)
    WID = sb("WID", [P, TT, H_IDX], F32, R + 65.5625)
    TOP8 = sb("TOP8", [P, 3, 8], F32, R + 65.75)
    STAT = sb("STAT", [P, 64], F32, R + 66)
    POSI, POSF = sb("POSI", [1, S], I32, R + 107), sb("POSF", [1, S], F32, R + 109)
    PICK = sb("PICK", [P, 6, P], F32, R + 67)
    COS16, SIN16, COS32, SIN32 = (sb(n, [P, S], F32, R + 70 + 2 * j)
                                  for j, n in enumerate(("COS16", "SIN16", "COS32", "SIN32")))
    QI, KI = sb("QI", [P, 2, S], F32, R + 78), sb("KI", [P, S], F32, R + 82)
    WORK = sb("WORK", [P, 9 * P], F32, R + 84)
    RL = sb("RL", [P, 2, S], F32, R + 89)
    MISC = sb("MISC", [P, S], F32, R + 93)
    XT = sb("XT", [P, 2, S], F32, R + 95)
    T1, T2 = sb("T1", [P, S], F32, R + 99), sb("T2", [P, S], F32, R + 101)
    RIN2 = sb("RIN2", [P, S], F32, R + 103)
    KRT = sb("KRT", [P, S], F32, R + 105)
    SQM = sb("SQM", [P, 2, S], F32, R + 84)

    s_c = [g.track(f"mixer1_{j}") for j in range(3)]
    wait(act, a_t[-1])
    pos_t = s_c[0].mark(act.dma_start(POSI[:, :], io["positions"]), by=16)
    const_into(INV[:, :], "inv", s_c[1])
    const_into(ROTQ[:, :], "rot_q", s_c[1])
    for j, name in enumerate(("rot32", "rot64", "pick_ki", "rot_ki", "pick_kr", "rot_kr")):
        const_t = const_into(PICK[:, j], name, s_c[1])
    ROT32, ROT64, PICK_KI, ROT_KI, PICK_KR, ROT_KR = (PICK[:, j] for j in range(6))

    def rotary_tables(pos_t):
        TURN = (6.28125, 0.0019350051879882812, 3.0199159819567529e-7)
        t = do(DV, [pos_t], dve.tensor_copy, POSF[:, :], POSI[:, :])
        wait(pe, latest("bank 7 read"))
        pos_t = do(PE, [t], pe.matmul, PS[:, 7], ONES[0:1, :], POSF[:, :], start=True, stop=True)
        ANG, TURNS = sb("ANG", [P, S], F32, R + 111), sb("TURNS", [P, S], I32, R + 113)
        TURNF, REST = sb("TURNF", [P, S], F32, R + 115), sb("REST", [P, 2, S], F32, R + 99)
        wait(dve, const_t)
        rest_free = [None, None]
        for j, (cos, sin) in enumerate(((COS16, SIN16), (COS32, SIN32))):
            t0 = do(DV, [pos_t], dve.tensor_scalar, ANG[:, :], PS[:, 7], INV[:, j:j + 1], None, ALU.mult)
            for n, (out, shift) in enumerate(((sin, 0.0), (cos, 0.25))):
                t = do(DV, [t0, rest_free[n]], dve.tensor_scalar, TURNS[:, :], ANG[:, :], 1.0 / (2 * math.pi), shift, ALU.mult, ALU.add)
                t = do(DV, [t], dve.tensor_copy, TURNF[:, :], TURNS[:, :])
                src = ANG[:, :]
                for part in TURN:
                    t = do(DV, [t], dve.scalar_tensor_tensor, out=REST[:, n], in0=TURNF[:, :], scalar=-part,
                           in1=src, op0=ALU.mult, op1=ALU.add)
                    src = REST[:, n]
                t = do(DV, [t], dve.tensor_scalar, REST[:, n], REST[:, n], shift * 2 * math.pi, None, ALU.add)
                t = do(DV, [t], dve.tensor_scalar, REST[:, n], REST[:, n], 3.1415925, -3.1415925, ALU.min, ALU.max)
                rest_free[n] = do(AC, [t], act.activation, out[:, :], REST[:, n], ACT.Sin)
        step("bank 7 read", t0)
        wait(dve, rest_free[1])
        do(DV, [rest_free[1]], dve.memset, SINQ[0:NOPE, :], 0.0)
        do(DV, [], dve.memset, COSQ[0:NOPE, :], 1.0)
        do(DV, [], dve.tensor_copy, COSQ[NOPE:D_QK, :], COS16[NOPE:D_QK, :])
        return do(DV, [], dve.tensor_copy, SINQ[NOPE:D_QK, :], SIN16[NOPE:D_QK, :])

    first_t = []
    for c in range(3):
        slot = take()
        first_t += two_blocks((2 * c, 2 * c + 1), slot, A, a_t)
        used(first_t[-1])
        feed()
        if c == 0:
            table_t = rotary_tables(pos_t)
    misc_t = do(AC, [first_t[5]], act.activation, MISC[:, :], PS[:, 5], ACT.Copy)
    step("bank 5 read", misc_t)

    def small_norm(blocks, n, bank, out):
        mm = None
        wait(pe, latest(f"bank {bank} read"))
        for q, b in enumerate(blocks):
            wait(act, latest(f"sqm{q % 2} used"))
            s = do(AC, [first_t[b]], act.activation, SQM[:, q % 2], PS[:, b], ACT.Square)
            mm = do(PE, [s], pe.matmul, PS[:, bank], ONES[:, :], SQM[:, q % 2], start=q == 0,
                    stop=q == len(blocks) - 1)
            step(f"sqm{q % 2} used", mm)
            sq_last[b] = s
        return root_mean(bank, mm, n, out)

    sq_last = {}
    rq_t = small_norm([0, 1, 2], Q_LORA, 6, RIN[:, :])
    rk_t = small_norm([3, 4], KV_LORA, 7, RIN2[:, :])

    def project_vb(c, r, slot, bank):
        wait(pe, latest(f"bank {bank} read"))
        n = 0
        for k in range(DB):
            cols = slice(k * 256, (k + 1) * 256)
            for wt, x in ((WHI, AHI), (WHI, ALO), (WLO, AHI)):
                m = pe.matmul(PS[:, bank, 0:256], x[:, k, r::4], wt[:, slot, cols], start=n == 0, stop=n == 23)
                n += 1
        t = do(AC, [PE.mark(m)], act.activation, VB[:, r, c * 256:(c + 1) * 256], PS[:, bank, 0:256], ACT.Copy)
        step(f"bank {bank} read", t)
        return t

    slot = take()
    lora_t, scaled_t = [], {}

    def scale_latent(b):
        r_t, r, gain, d = (rq_t, RIN, "g_cq", b) if b < 3 else (rk_t, RIN2, "g_ckv", b - 3)
        wait(dve, latest(f"xt{b % 2} used"))
        scaled_t[b] = do(DV, [r_t, sq_last[b]], dve.scalar_tensor_tensor, out=XT[:, b % 2], in0=PS[:, b],
                         scalar=vec(gain, d, 1), in1=r[:, :], op0=ALU.mult, op1=ALU.mult)
        step(f"bank {b} read", scaled_t[b])

    scale_latent(0)
    for b in range(5):
        hi, lo, d = (CQH, CQL, b) if b < 3 else (CKH, CKL, b - 3)
        if b < 4:
            scale_latent(b + 1)
        lora_t.append(split_from(XT[:, b % 2], hi[:, d], lo[:, d], [scaled_t[b]]))
        step(f"xt{b % 2} used", lora_t[-1])
        if b < 4:
            project_vb(0, b, slot, 5 + b % 2)
    used(PE.now())
    feed()
    CQ = [(CQH[:, k], CQL[:, k]) for k in range(3)]
    CK = [(CKH[:, k], CKL[:, k]) for k in range(2)]

    def rotate(x, x_t, rot_w, bank, cos, sin, out, rows=slice(0, P), before=(), rhs=None, n=P):
        wait(pe, latest(f"bank {bank} read"))
        mm = do(PE, [x_t, const_t], pe.matmul, PS[0:n, bank], rot_w, x if rhs is None else rhs, start=True, stop=True)
        wait(dve, latest("t12 used"))
        a = do(DV, [x_t, table_t, mm, *before], dve.tensor_tensor, T1[rows, :], x[rows, :], cos[rows, :], ALU.mult)
        b = do(DV, [], dve.tensor_tensor, T2[rows, :], PS[rows, bank], sin[rows, :], ALU.mult)
        step(f"bank {bank} read", b)
        c = do(DV, [a, b], dve.tensor_tensor, out, T1[rows, :], T2[rows, :], ALU.add)
        step("t12 used", c)
        return c

    slot = take()
    wait(pe, *lora_t)
    qi_t = []
    iq = [linear(f, slot, f * P, 2 * P, CQ) for f in range(2)]
    used(iq[1])
    for f in range(2):
        wait(act, latest(f"xt{f} used"))
        t = do(AC, [iq[f]], act.activation, XT[:, f], PS[:, f], ACT.Copy)
        step(f"bank {f} read", t)
        qi_t.append(rotate(XT[:, f], t, ROT32, 2 + f, COS16, SIN16, QI[:, f]))
        step(f"xt{f} used", qi_t[-1])
    feed()
    wait(pe, latest("bank 4 read"))
    t = do(PE, [misc_t, const_t], pe.matmul, PS[:, 4], PICK_KI, MISC[:, :], start=True, stop=True)
    ki_t = rotate(PS[:, 4], t, ROT_KI, 5, COS16, SIN16, KI[:, :], rhs=MISC[:, :])
    step("bank 4 read", ki_t)
    wait(pe, latest("bank 6 read"))
    t = do(PE, [], pe.matmul, PS[:, 6], PICK_KR, MISC[:, :], start=True, stop=True)
    kr_t = rotate(PS[:, 6], t, ROT_KR, 7, COS16, SIN16, KRT[NOPE:D_QK, :], rows=slice(NOPE, D_QK), rhs=MISC[:, :])
    step("bank 6 read", kr_t)
    wait(pe, latest("bank 5 read"))
    for i in range(TT):
        t = pe.transpose(PS[:, 5, i * P:(i + 1) * P], MISC[:, i * P:(i + 1) * P], IDENT[:, :])
    t = PE.mark(t)
    wid_t = do(AC, [t], act.activation, WID[:, :, :],
               PS[:, 5].rearrange("p (i c) -> p i c", i=TT)[:, :, 64:64 + H_IDX], ACT.Copy, scale=H_IDX ** -0.5)
    step("bank 5 read", wid_t)

    def tile_cols(i):
        at = (0, 2 * P, 5 * P)[i - 1]
        return slice(at, at + (i + 1) * P)

    wait(pe, *qi_t, ki_t)
    work_t, n_u = {}, 0
    for h in range(H_IDX):
        rows = slice(32 * (h % 4), 32 * (h % 4) + 32)
        for i in range(1, TT):
            n, bank = (i + 1) * P, n_u % 4
            wait(pe, latest(f"bank {bank} read"))
            mm = do(PE, [], pe.matmul, PS[:, bank, 0:n], QI[rows, h // 4, i * P:(i + 1) * P],
                    KI[rows, 0:n], start=True, stop=True)
            wait(act, latest(f"rl{n_u % 2} used"))
            r = do(AC, [mm], act.activation, RL[:, n_u % 2, 0:n], PS[:, bank, 0:n], ACT.Relu, scale=32 ** -0.5)
            step(f"bank {bank} read", r)
            dst, wcol = WORK[:, tile_cols(i)], WID[:, i, h:h + 1]
            if h == 0:
                work_t[i] = do(DV, [r, wid_t, latest("sqm0 used"), latest("sqm1 used")],
                               dve.tensor_scalar, dst, RL[:, n_u % 2, 0:n], wcol, None, ALU.mult)
            else:
                work_t[i] = do(DV, [r, work_t[i]], dve.scalar_tensor_tensor, out=dst, in0=RL[:, n_u % 2, 0:n],
                               scalar=wcol, in1=dst, op0=ALU.mult, op1=ALU.add)
            step(f"rl{n_u % 2} used", work_t[i])
            n_u += 1
    STRUCK = -3e38
    for i in range(1, TT):
        diag = WORK[:, tile_cols(i)][:, i * P:(i + 1) * P]
        work_t[i] = do(DV, [work_t[i]], dve.tensor_tensor, diag, diag, CAUSAL[:, :], ALU.add)
    for _ in range(TOPK // 8):
        for i in range(1, TT):
            src = WORK[:, tile_cols(i)]
            work_t[i] = do(DV, [work_t[i]], dve.max, TOP8[:, i - 1], src)
        for i in range(1, TT):
            src = WORK[:, tile_cols(i)]
            work_t[i] = do(DV, [work_t[i]], dve.match_replace, src, TOP8[:, i - 1], src, STRUCK)
    do(DV, [], dve.tensor_copy, SEL[:, 0:P], CAUSAL[:, :])
    for i in range(1, TT):
        src = WORK[:, tile_cols(i)]
        at = tile_cols(i).start + P
        sel_t = do(DV, [work_t[i]], dve.tensor_scalar, SEL[:, at:at + (i + 1) * P], src, -2e38, NEG,
                   ALU.is_gt, ALU.mult)

    wait(pe, AC.now())
    with wloop(3, 2) as i:
        for c in range(2):
            slot = take()
            mm = [linear(4 + 2 * c + f, slot, f * P, 2 * P, A) for f in range(2)]
            used(mm[1])
            for f in range(2):
                qkb_t = do(AC, [mm[f]], act.activation,
                           QKB[:, bass.ds(i * 4 + (2 * c + f), 1)].rearrange("p a s -> p (a s)"),
                           PS[:, 4 + 2 * c + f], ACT.Copy)
                step(f"bank {4 + 2 * c + f} read", qkb_t)
            feed()
    for c in (1, 2):
        slot = take()
        for r in range(4):
            vb_t = project_vb(c, r, slot, (4 * c + r) % 8)
        used(PE.now())
        feed()
    wait(pe, qkb_t, table_t)
    wait(dve, qkb_t)
    meet()
    with g.loop(6) as i:
        for f in range(2):
            blk = QKB[:, bass.ds(i * 2 + f, 1)].rearrange("p a s -> p (a s)")
            wait(pe, latest(f"bank {f} read"))
            mm = do(PE, [], pe.matmul, PS[:, f], ROT64, blk, start=True, stop=True)
            wait(dve, latest("t12 used"))
            a = do(DV, [mm], dve.tensor_tensor, T1[:, :], blk, COS32[:, :], ALU.mult)
            b = do(DV, [], dve.tensor_tensor, T2[:, :], PS[:, f], SIN32[:, :], ALU.mult)
            step(f"bank {f} read", b)
            qkr_t = do(DV, [a, b], dve.tensor_tensor, blk, T1[:, :], T2[:, :], ALU.add)
            step("t12 used", qkr_t)

    QF, KF = sb("QF", [P, 2, S], F32, R + 67), sb("KF", [P, 2, S], F32, R + 71)
    VP = sb("VP", [P, TT, P], F32, R + 75)
    SM = sb("SM", [P, 2, 10 * P], F32, R + 77)
    PT = sb("PT", [P, TT, S], F32, R + 87)
    OAH, OAL = sb("OAH", [P, 4, S], F32R, R + 103), sb("OAL", [P, 4, S], F32R, R + 111)
    wait(dve, kr_t, sel_t, qkr_t.last())
    for a in range(2):
        kf_t = do(DV, [], dve.tensor_copy, KF[NOPE:D_QK, a], KRT[NOPE:D_QK, :])
    phase2_t = kf_t
    wait(act, phase2_t)


    def causal_softmax(SM, STAT, head, q, k, mask, scale, banks, waits, mask_t=(), key_bias=None):
        col, st = 0, STAT[:, head * 32:(head + 1) * 32]
        low, sums, inv = st[:, 0:4], st[:, 4:8], st[:, 8:12]
        wait(dve, latest(f"sm{head} used"))
        parts = []
        for i in range(TT):
            n = (i + 1) * P
            wait(pe, latest(f"bank {banks[i]} read"))
            mm = do(PE, waits, pe.matmul, PS[:, banks[i], 0:n], q[:, i * P:(i + 1) * P], k[:, 0:n], start=True,
                    stop=key_bias is None)
            if key_bias:
                mm = do(PE, [], pe.matmul, PS[:, banks[i], 0:n], key_bias[0], key_bias[1][:, 0:n], start=False,
                        stop=True)
            sm = SM[:, head, col:col + n]
            do(DV, [mm, *mask_t], dve.memset, st[:, 12 + i:13 + i], 0.0)
            t = do(DV, [], dve.tensor_tensor_reduce, sm, PS[:, banks[i], 0:n], mask[:, col:col + n], -scale,
                   3e38, ALU.add, ALU.min, low[:, i:i + 1])
            step(f"bank {banks[i]} read", t)
            e = do(AC, [t], act.activation, sm, sm, ACT.Exp, bias=low[:, i:i + 1], scale=-1.0,
                   accum_out=sums[:, i:i + 1])
            parts.append((e, sm, n, col))
            col += n
        r = None
        for i, (e, sm, n, c) in enumerate(parts):
            r = do(DV, [e], dve.reciprocal, inv[:, i:i + 1], sums[:, i:i + 1])
            parts[i] = (do(DV, [r], dve.tensor_scalar, sm, sm, inv[:, i:i + 1], None, ALU.mult), sm, n, c)
        return parts

    def transposed(PT, parts, banks, head):
        wait(act, latest("pt used"))
        for i, (t, sm, n, c) in enumerate(parts):
            wait(pe, latest(f"bank {banks[i]} read"))
            wait(pe, t)
            for j in range(i + 1):
                m = pe.transpose(PS[:, banks[i], j * P:(j + 1) * P], sm[:, j * P:(j + 1) * P], IDENT[:, :])
            m = PE.mark(m)
            pt_t = do(AC, [m], act.activation, PT[:, 0:i + 1, i * P:(i + 1) * P],
                      PS[:, banks[i], 0:n].rearrange("p (j q) -> p j q", q=P), ACT.Copy)
            step(f"bank {banks[i]} read", pt_t)
        step(f"sm{head} used", m)
        return pt_t

    def weighted_values(PT, out, v, pt_t, v_t):
        wait(pe, pt_t, v_t)
        for j in range(TT):
            m = pe.matmul(out[:, j * P:S], v[j], PT[:, j, j * P:S], start=j == 0, stop=j == TT - 1)
        m = PE.mark(m)
        step("pt used", m)
        return m

    VP2 = nc.alloc_sbuf_tensor_at("VP2", [P, TT, P], F32, offset=512 + 102 * 1024)

    def project_pair(VP, name):
        slot = take()
        q_mm = [linear(f, slot, f * D_QK, 2 * D_QK, CQ, width=D_QK, rows=D_QK) for f in range(2)]
        k_mm = linear(2, slot, 576, P, CK)
        wait(pe, latest("bank 3 read"))
        for t in range(TT):
            n = 0
            for k in range(2):
                for wt, x in ((WHI, CKH), (WHI, CKL), (WLO, CKH)):
                    m = pe.matmul(PS[:, 3, t * P:(t + 1) * P], x[:, k, t * P:(t + 1) * P],
                                  wt[:, slot, 832 + k * P:832 + (k + 1) * P], start=n == 0, stop=n == 5)
                    n += 1
        v_mm = PE.mark(m)
        used(v_mm)
        q_t = []
        for f in range(2):
            wait(act, latest(f"xt{f} used"))
            t = do(AC, [q_mm[f]], act.activation, XT[0:D_QK, f], PS[0:D_QK, f], ACT.Copy)
            step(f"bank {f} read", t)
            wait(dve, latest(f"qf{f} used"))
            q_t.append(rotate(XT[:, f], t, ROTQ[0:D_QK, 0:D_QK], 4 + f, COSQ, SINQ, QF[0:D_QK, f],
                              rows=slice(0, D_QK), rhs=XT[0:D_QK, f], n=D_QK))
            step(f"xt{f} used", q_t[-1])
        for f in range(2):
            wait(act, latest(f"kf{f} used"))
            k_t = do(AC, [k_mm], act.activation, KF[0:NOPE, f], PS[f * NOPE:(f + 1) * NOPE, 2], ACT.Copy)
        step("bank 2 read", k_t)
        wait(act, latest(name + " used"))
        v_t = do(AC, [v_mm], act.activation, VP[:, :, :], PS[:, 3].rearrange("p (t c) -> p t c", c=P), ACT.Copy)
        step("bank 3 read", v_t)
        feed()
        return q_t, k_t, v_t

    def weigh_pair(q_t, k_t):
        parts = []
        for f in range(2):
            parts.append(causal_softmax(SM, STAT, f, QF[0:D_QK, f], KF[0:D_QK, f], SEL, D_QK ** -0.5,
                                        ((0, 1, 2, 3), (6, 7, 4, 5))[f], [q_t[f], k_t, kf_t]))
            step(f"qf{f} used", PE.now())
            step(f"kf{f} used", PE.now())
        return parts

    def sum_pair(parts, VP, name, v_t, pair):
        wait(pe, latest("bank 0 read"))
        for f in range(2):
            pt_t = transposed(PT, parts[f], ((6, 7, 4, 5), (1, 2, 3, 6))[f], f)
            o_mm = weighted_values(PT, PS[f * NOPE:(f + 1) * NOPE, 0], [VP[:, j, f * NOPE:(f + 1) * NOPE] for j in range(TT)],
                                   pt_t, v_t)
        step(name + " used", o_mm)
        blk = bass.ds(pair, 1)
        hi, lo = (x[:, blk].rearrange("p a s -> p (a s)") for x in (OAH, OAL))
        t = do(AC, [o_mm], act.activation, hi, PS[:, 0], ACT.Copy)
        t = do(DV, [t], dve.tensor_tensor, lo, PS[:, 0], hi.bitcast(F32), ALU.subtract)
        step("bank 0 read", t)
        return t, o_mm

    meet()
    tables("exp")
    with wloop(2, 2) as i:
        q_t, k_t, v_t = project_pair(VP, "vp")
        parts = weigh_pair(q_t, k_t)
        q_t, k_t, v2_t = project_pair(VP2, "vp2")
        sum_pair(parts, VP, "vp", v_t, i * 2)
        parts = weigh_pair(q_t, k_t)
        oa_t, o_mm = sum_pair(parts, VP2, "vp2", v2_t, i * 2 + 1)

    MASKB = sb("MASKB", [P, 9, P], F32, R + 67)
    SMB = sb("SMB", [P, 2, 6 * P], F32, R + 77)
    PTB = sb("PTB", [P, 2, 6 * P], F32, R + 87)
    OBH, OBL = sb("OBH", [P, 2, S], F32R, R + 0), sb("OBL", [P, 2, S], F32R, R + 4)
    phase3 = [oa_t.last(), o_mm.last()]
    wait(act, *phase3)
    wait(dve, *phase3)
    c = CONST_AT["near0"]
    mask_t = s_c[2].mark(act.dma_start(MASKB[:, :, :], io["consts"][:, c:c + 9 * P].rearrange("p (m k) -> p m k", k=P)), by=16)
    wait(pe, qkr_t.last(), vb_t)

    def dilated_softmax(u, hp, r, f):
        rows = slice(f * 64, f * 64 + 64)
        b0, b1 = 2 * u, 2 * u + 1
        st = STAT[:, 32 * u:32 * u + 32]

        def q_of(grp):
            return QKB[rows, 2 * grp + hp, r::4]

        def k_of(grp, res):
            return QKB[rows, 6 + 2 * grp + hp, res::4]

        wait(pe, latest(f"bank {b0} read"), latest(f"bank {b1} read"))
        for j in range(4):
            m = pe.matmul(PS[:, b0, j * P:(j + 1) * P], q_of(0), k_of(0, j), start=True, stop=True)
        for grp in (1, 2):
            m = pe.matmul(PS[:, b1, (grp - 1) * P:grp * P], q_of(grp), k_of(grp, r), start=True, stop=True)
        mm = PE.mark(m)
        wait(dve, latest(f"smb{u} used"))
        t = do(DV, [mm, mask_t], dve.tensor_tensor_reduce, SMB[:, u, 0:S], PS[:, b0],
               MASKB[:, 3 - r:7 - r].rearrange("p m k -> p (m k)"), -0.125, 3e38, ALU.add, ALU.min, st[:, 0:1])
        step(f"bank {b0} read", t)
        t = do(DV, [t], dve.tensor_tensor_reduce, SMB[:, u, S:S + 2 * P], PS[:, b1, 0:2 * P],
               MASKB[:, 7:9].rearrange("p m k -> p (m k)"), -0.125, st[:, 0:1], ALU.add, ALU.min, st[:, 1:2])
        step(f"bank {b1} read", t)
        return do(AC, [t], act.activation, SMB[:, u], SMB[:, u], ACT.Exp, bias=st[:, 1:2], scale=-1.0,
                  accum_out=st[:, 2:3])

    def normalised(u, e):
        st = STAT[:, 32 * u:32 * u + 32]
        t = do(DV, [e], dve.reciprocal, st[:, 3:4], st[:, 2:3])
        return do(DV, [t], dve.tensor_scalar, SMB[:, u], SMB[:, u], st[:, 3:4], None, ALU.mult)

    def turned(u, p_t):
        bt = 4 + u
        wait(pe, latest(f"bank {bt} read"), p_t)
        for j in range(4):
            m = pe.transpose(PS[:, bt, j * P:(j + 1) * P], SMB[:, u, j * P:(j + 1) * P], IDENT[:, :])
        m = PE.mark(m)
        wait(act, latest(f"ptb{u} used"))
        t = do(AC, [m], act.activation, PTB[:, u, 0:S], PS[:, bt], ACT.Copy)
        step(f"bank {bt} read", t)
        wait(pe, latest("bank 6 read"))
        for j in range(2):
            m = pe.transpose(PS[:, 6, j * P:(j + 1) * P], SMB[:, u, S + j * P:S + (j + 1) * P], IDENT[:, :])
        m = PE.mark(m)
        step(f"smb{u} used", m)
        t = do(AC, [m], act.activation, PTB[:, u, S:S + 2 * P], PS[:, 6, 0:2 * P], ACT.Copy)
        step("bank 6 read", t)
        return t

    def dilated_values(u, hp, r, f, pt_t):
        wait(pe, pt_t)
        if r == 0 and f == 0:
            wait(pe, latest("bank 7 read"))
        for j in range(6):
            grp, res = (0, j) if j < 4 else (j - 3, r)
            c = grp * 256 + (2 * hp + f) * 64
            m = pe.matmul(PS[f * 64:f * 64 + 64, 7, r * P:(r + 1) * P], VB[:, res, c:c + 64],
                          PTB[:, u, j * P:(j + 1) * P], start=j == 0, stop=j == 5)
        o_mm = PE.mark(m)
        step(f"ptb{u} used", o_mm)
        if r == 3 and f == 1:
            src = PS[:, 7].rearrange("p (r a) -> p a r", r=4)
            dst = [x[:, hp].rearrange("p (a r) -> p a r", r=4) for x in (OBH, OBL)]
            t = do(AC, [o_mm], act.activation, dst[0], src, ACT.Copy)
            t = do(DV, [t], dve.tensor_tensor, dst[1], src, dst[0].bitcast(F32), ALU.subtract)
            step("bank 7 read", t)

    units = [(hp, r, f) for hp in range(2) for r in range(4) for f in range(2)]
    e_t, p_t, pt_t = {}, {}, {}
    for n in range(len(units) + 2):
        if n < len(units):
            e_t[n] = dilated_softmax(n % 2, *units[n])
        if 0 < n <= len(units):
            pt_t[n - 1] = turned((n - 1) % 2, p_t[n - 1])
        if n < len(units):
            p_t[n] = normalised(n % 2, e_t[n])
        if n > 1:
            dilated_values(n % 2, *units[n - 2], pt_t[n - 2])
    ob_t = latest("bank 7 read")
    OA = [(OAH[:, k], OAL[:, k]) for k in range(4)]
    OB = [(OBH[:, k], OBL[:, k]) for k in range(2)]

    ZH, ZL = sb("ZH", [P, DB, S], F32R, R + 20), sb("ZL", [P, DB, S], F32R, R + 36)
    SG = sb("SG", [P, 2, S], F32, R + 77)
    TZ = sb("TZ", [P, 2, S], F32, R + 81)
    def gated_sum(n, a_in, rhs_a, rhs_b, SG, TZ, ZH, ZL, gate_bias=None):
        meet()
        tables("sigmoid")
        with wloop(n, 2) as i:
            sg_t, mm = [], []
            for f, rhs in enumerate((rhs_b, rhs_a)):
                slot = take()
                gate_mm = linear(f, slot, 0, P, a_in)
                mm.append(linear(3 - f, slot, D, P, rhs))
                used(mm[f])
                wait(act, latest(f"sg{f} used"))
                bias = 0.0 if gate_bias is None else VEC[:, bass.ds(i + (gate_bias + f * DB), 1)]
                sg_t.append(do(AC, [gate_mm], act.activation, SG[:, f], PS[:, f], ACT.Sigmoid, bias=bias))
                step(f"bank {f} read", sg_t[f])
                feed()
            ub, ua = mm
            t = []
            for f, mm in enumerate((ua, ub)):
                wait(dve, latest(f"tz{f} used"))
                t.append(do(DV, [mm, sg_t[f]], dve.tensor_tensor, TZ[:, f], PS[:, 2 + f], SG[:, f], ALU.mult))
                step(f"bank {2 + f} read", t[f])
                step(f"sg{f} used", t[f])
            s = do(DV, t, dve.tensor_tensor, TZ[:, 0], TZ[:, 0], TZ[:, 1], ALU.add)
            step("tz1 used", s)
            blk = bass.ds(i, 1)
            h = do(AC, [s], act.activation, ZH[:, blk], TZ[:, 0:1], ACT.Copy)
            z_t = do(DV, [h], dve.tensor_tensor, ZL[:, blk], TZ[:, 0:1], ZH[:, blk].bitcast(F32), ALU.subtract)
            step("tz0 used", z_t)
        return z_t

    wait(act, ob_t)
    wait(pe, oa_t.last(), ob_t)
    z_t = gated_sum(DB, A, OA, OB, SG, TZ, ZH, ZL)

    def square_linear(rhs, ready, sq_at, y_at, between=None):
        u = g.next_name()
        Y, SQ = sb(f"Y{u}", [P, DB, S], F32, R + y_at), sb(f"SQ{u}", [P, 2, S], F32, R + sq_at)
        wait(pe, *ready)
        wait(act, *ready)
        wait(dve, *ready)
        tables("natural_log_exp")
        outs = []
        for c in range(4):
            slot = take()
            for f in range(2):
                d = 2 * c + f
                mm = linear(d, slot, f * P, 2 * P, rhs)
                take_output(Y, SQ, d, d, mm, outs)
            used(mm)
            if c < 3:
                feed()
            if c == 1 and between:
                between()
        return Y, [y for _, y, _ in outs]

    Z = [(ZH[:, k], ZL[:, k]) for k in range(DB)]
    Y, y_t = square_linear(Z, [z_t.last()], 88, 98)
    x_t = residual(Y, y_t, 0, coef(3))
    a_t = prenorm(x_t, coef(4), mod(6))
    x_t = ffn(a_t, coef(5))
    a_t = prenorm(x_t, vec("ffn1_pre_g_2"))
    x_t = ffn(a_t, coef(6))

    OBH2, OBL2 = sb("OBH2", [P, DB, S], F32R, R), sb("OBL2", [P, DB, S], F32R, R + 16)
    OAR = sb("OAR", [P, HG, S], F32, R + 32)
    FQ, FK, FVF = (sb(n, [P, S], F32, R + 48 + 2 * j) for j, n in enumerate(("FQ", "FK", "FVF")))
    FV = sb("FV", [P, TT, P], F32, R + 54)
    MASKC = sb("MASKC", [P, 10 * P], F32, R + 56)
    NEGC, PICKH = sb("NEGC", [P, S], F32, R + 61), sb("PICKH", [P, P], F32, R + 63)
    LEVELS = sb("LEVELS", [P, 8, P], F32, R + 64)
    RESET = sb("RESET", [P, S], F32, R + 68)
    XC, SIG = sb("XC", [P, 2, S], F32, R + 70), sb("SIG", [P, 2, S], F32, R + 74)
    XG, SIGG, GS, QH, KK, FG, LF, B = (sb(n, [P, S], F32, R + 78 + 2 * j) for j, n in
                                       enumerate(("XG", "SIGG", "GS", "QH", "KK", "FG", "LF", "B")))
    E = sb("E", [P, 3, S], F32, R + 94)
    KS, QS, IFM = (sb(n, [P, S], F32, R + 100 + 2 * j) for j, n in enumerate(("KS", "QS", "IFM")))
    ITM, KST = sb("ITM", [P, TT, P], F32, R + 106), sb("KST", [P, TT, P], F32, R + 108)
    STATE = sb("STATE", [P, TT - 1, P], F32, R + 110)
    PAIRS = sb("PAIRS", [P, TT, P], F32, R + 112)
    SQO = sb("SQO", [P, 2, S], F32, R + 114)
    DEC, SCR = sb("DEC", [P, TT], F32, R + 118), sb("SCR", [P, 32], F32, R + 118.125)
    LB, OML = sb("LB", [P, HG], F32, R + 118.25), sb("OML", [P, HG], F32, R + 118.3125)
    FBIAS = sb("FBIAS", [P, 1], F32, R + 118.375)

    s_c2 = [g.track(f"mixer2_{j}") for j in range(2)]
    a_t = prenorm(x_t, vec("mix_pre_g_2"))
    wait(act, a_t[-1])
    const2_t = s_c2[0].mark(act.dma_start(FBIAS[0:FOX, :], io["fox_bias"]), by=16)
    const_into(RESET[:, :], "reset", s_c2[1])
    levels_t = const_into(LEVELS[:, :, :].rearrange("p a b -> p (a b)"), "levels", s_c2[1])
    wait(dve, const2_t)

    slot = take()
    qf_mm = two_blocks((4, 5), slot, A, a_t)
    used(qf_mm[1])
    feed()
    slot = take()
    fb_mm = linear(0, slot, 0, P, A)
    used(fb_mm)
    feed()
    x_f, low_f, t_f = E[0:FOX, 0], E[0:FOX, 1], E[0:FOX, 2]
    t = do(DV, [fb_mm], dve.tensor_scalar, x_f, PS[0:FOX, 0], FBIAS[0:FOX, :], None, ALU.add)
    step("bank 0 read", t)
    t = do(DV, [t], dve.tensor_scalar, low_f, x_f, 0.0, None, ALU.min)
    t = do(DV, [t], dve.scalar_tensor_tensor, out=t_f, in0=low_f, scalar=2.0, in1=x_f, op0=ALU.mult, op1=ALU.subtract)
    t = do(AC, [t], act.activation, t_f, t_f, ACT.Exp)
    t = do(AC, [t], act.activation, t_f, t_f, ACT.Ln, bias=ONES[0:FOX, 0:1])
    t = do(DV, [t], dve.tensor_tensor, x_f, low_f, t_f, ALU.subtract)
    s = do(DV, [t], dve.memset, t_f, 1.0)
    t = do(DV, [t, s], dve.tensor_tensor_scan, low_f, t_f, x_f, 0.0, ALU.mult, ALU.add)
    negc_t = do(DV, [t], dve.tensor_scalar, NEGC[0:FOX, :], low_f, -math.sqrt(P), None, ALU.mult)

    t = do(DV, [], dve.tensor_tensor, LB[:, :], vec("hg_lb_logits_2", DB), vec("hg_lb_logits_2"), ALU.subtract)
    t = do(AC, [t], act.activation, LB[:, :], LB[:, :], ACT.Exp)
    t = do(DV, [t], dve.tensor_scalar, LB[:, :], LB[:, :], 1.0, None, ALU.add)
    t = do(DV, [t], dve.reciprocal, LB[:, :], LB[:, :])
    t = do(DV, [t], dve.tensor_scalar, OML[:, :], LB[:, :], -1.0, 1.0, ALU.mult, ALU.add)
    do(DV, [], dve.memset, SSQ[:, :], 0.0)
    t = do(DV, [], dve.memset, PAIRS[:, :, :], 0.0)
    s = do(DV, [], dve.memset, MASKC[:, :], 0.0)
    for n in (1, 3, 6, 10):
        t = do(DV, [s], dve.tensor_copy, MASKC[:, (n - 1) * P:n * P], CAUSAL[:, :])
    wait(dve, t, negc_t, levels_t)
    wait(act, t, negc_t)

    settled = [0]

    def settle(*waits):
        settled[0] += 1
        do(DV, waits, dve.memset, SCR[:, settled[0] % 32:settled[0] % 32 + 1], 0.0)

    def projection(banks, slot):
        marks = []

        def work():
            for f, bank in enumerate(banks):
                wait(pe, latest(f"bank {bank} read"))
                for q in range(DB):
                    at = q * 2 * P + f * P
                    for r, (wt, x) in enumerate(((WHI, A[q][0]), (WHI, A[q][1]), (WLO, A[q][0]))):
                        m = pe.matmul(PS[:, bank], wt[:, slot, at:at + P], x, start=q == 0 and r == 0,
                                      stop=q == DB - 1 and r == 2)
                        if q == DB - 1 and r == 2:
                            marks.append(PE.mark(m))
                            if f:
                                used(marks[1])
                        yield

        steps = work()

        def run(n=2 * 3 * DB + 1):
            for _ in range(n):
                next(steps, None)

        return run, marks

    FLOOR = -80.0

    def sigmoid(out, x, waits):
        t = do(AC, waits, act.activation, out, x, ACT.Exp, scale=-1.0)
        t = do(AC, [t], act.activation, out, out, ACT.Ln, bias=ONES[:, 0:1])
        return do(AC, [t], act.activation, out, out, ACT.Exp, scale=-1.0)

    def take_qf(marks):
        wait(dve, latest("xc used"))
        t = do(DV, marks, dve.tensor_scalar, XC[:, :, :], PS[:, 4:6], FLOOR, None, ALU.max)
        step("bank 4 read", t)
        step("bank 5 read", t)
        step("xc ready", t)

    def hgrn_head(h, last):
        slot = take()
        ig = [linear(f, slot, f * P, 2 * P, A) for f in range(2)]
        used(ig[1])
        wait(act, latest("xc ready"), latest("sig used"))
        t = sigmoid(SIG[:, :, :], XC[:, :, :], [])
        wait(dve, latest("qk used"))
        q_t = do(DV, [t], dve.tensor_tensor, QH[:, :], XC[:, 0], SIG[:, 0], ALU.mult)
        step("xc used", q_t)
        t = do(DV, [], dve.tensor_scalar, FG[:, :], SIG[:, 1], OML[:, bass.ds(h, 1)], LB[:, bass.ds(h, 1)], ALU.mult, ALU.add)
        step("sig used", t)
        k_t = do(DV, [t], dve.tensor_scalar, KK[:, :], FG[:, :], -1.0, 1.0, ALU.mult, ALU.add)
        t = do(AC, [t], act.activation, LF[:, :], FG[:, :], ACT.Ln)
        b_t = do(DV, [t], dve.tensor_tensor_scan, B[:, :], RESET[:, :], LF[:, :], 0.0, ALU.mult, ALU.add)
        b4 = B[:, :].rearrange("p (c s) -> p c s", s=P)
        wait(dve, latest("ks used"))
        t = do(DV, [b_t], dve.tensor_tensor, KS[:, :].rearrange("p (c s) -> p c s", s=P),
               b4[:, :, P - 1:P].to_broadcast([P, TT, P]), b4, ALU.subtract)
        t = do(AC, [t], act.activation, KS[:, :], KS[:, :], ACT.Exp)
        ks_t = do(DV, [t, k_t], dve.tensor_tensor, KS[:, :], KS[:, :], KK[:, :], ALU.mult)
        wait(act, latest("qs used"))
        do(AC, [], act.activation, DEC[:, :].rearrange("p (c a) -> p c a", a=1), b4[:, :, P - 1:P], ACT.Exp)
        t = do(AC, [], act.activation, QS[:, :], B[:, :], ACT.Exp)
        qs_t = do(DV, [t, q_t], dve.tensor_tensor, QS[:, :], QS[:, :], QH[:, :], ALU.mult)
        if last:
            run, marks = (lambda n=0: None), None
        else:
            slot = take()
            run, marks = projection((4, 5), slot)

        def pairs(n, left, right, waits):
            bank = 6 + n % 2
            wait(pe, latest(f"bank {bank} read"))
            wait(pe, *waits)
            for c in range(TT):
                m = pe.matmul(PS[:, bank, c * P:(c + 1) * P], left[:, c * P:(c + 1) * P],
                              right[:, c * P:(c + 1) * P], start=True, stop=True)
            return PE.mark(m)

        def keep(n, mm, before):
            settle(mm, before)
            t = do(DV, [], dve.copy_predicated, PAIRS[:, :, :],
                   LEVELS[:, n:n + 1].bitcast(mybir.dt.uint32).to_broadcast([P, TT, P]),
                   PS[:, 6 + n % 2].rearrange("p (c t) -> p c t", t=P))
            step(f"bank {6 + n % 2} read", t)
            return t

        wait(dve, latest("pairs used"))
        mm = pairs(0, KK[:, :], QH[:, :], [q_t, k_t])
        run(5)
        kept, e_t, mm, exp_t = None, {}, {0: mm}, {}
        for n in range(1, 10):
            if n < 8:
                half = 1 << (n - 1)
                bl = B[:, :].rearrange("p (m two l) -> p m two l", two=2, l=half)
                el = E[:, n % 3].rearrange("p (m two l) -> p m two l", two=2, l=half)
                anchor = bl[:, :, 0, half - 1:half].to_broadcast([P, S // (2 * half), half])
                wait(dve, latest(f"e{n % 3} used"))
                do(DV, [b_t], dve.tensor_tensor, el[:, :, 0], anchor, bl[:, :, 0], ALU.subtract)
                t = do(DV, [], dve.tensor_tensor, el[:, :, 1], bl[:, :, 1], anchor, ALU.subtract)
                exp_t[n] = do(AC, [t], act.activation, E[:, n % 3], E[:, n % 3], ACT.Exp)
            if 0 < n - 1 < 8:
                o, half = n - 1, 1 << (n - 2)
                el, kl, ql = (x.rearrange("p (m two l) -> p m two l", two=2, l=half)
                              for x in (E[:, o % 3], KK[:, :], QH[:, :]))
                do(DV, [exp_t[o], k_t], dve.tensor_tensor, el[:, :, 0], el[:, :, 0], kl[:, :, 0], ALU.mult)
                t = do(DV, [], dve.tensor_tensor, el[:, :, 1], el[:, :, 1], ql[:, :, 1], ALU.mult)
                mm[o] = pairs(o, E[:, o % 3], E[:, o % 3], [t])
                step(f"e{o % 3} used", mm[o])
                run(5)
            if n - 2 >= 0:
                kept = keep(n - 2, mm[n - 2], kept or q_t)
            if n == 2:
                wait(pe, latest("bank 2 read"), ks_t)
                for c in range(TT - 1):
                    m = pe.transpose(PS[:, 2, c * P:(c + 1) * P], KS[:, c * P:(c + 1) * P], IDENT[:, :])
                t = PE.mark(m)
                step("ks used", t)
                wait(act, latest("kst used"))
                kst_t = do(AC, [t], act.activation, KST[:, 0:TT - 1], PS[:, 2, 0:(TT - 1) * P].rearrange("p (c t) -> p c t", t=P), ACT.Copy)
                step("bank 2 read", kst_t)
                wait(act, latest("ifm used"))
                i_t = do(AC, [ig[0]], act.activation, IFM[:, :], PS[:, 0], ACT.Copy)
                step("bank 0 read", i_t)
                wait(dve, latest("gs used"))
                xg_t = do(DV, [ig[1]], dve.tensor_scalar, XG[:, :], PS[:, 1], FLOOR, None, ALU.max)
                step("bank 1 read", xg_t)
            if n == 3:
                wait(pe, latest("bank 3 read"), i_t)
                for c in range(TT):
                    m = pe.transpose(PS[:, 3, c * P:(c + 1) * P], IFM[:, c * P:(c + 1) * P], IDENT[:, :])
                t = PE.mark(m)
                step("ifm used", t)
                wait(act, latest("itm used"))
                it_t = do(AC, [t], act.activation, ITM[:, :, :], PS[:, 3].rearrange("p (c t) -> p c t", t=P), ACT.Copy)
                step("bank 3 read", it_t)
                feed()
            if n == 4:
                wait(pe, latest("bank 2 read"), kst_t, it_t)
                for c in range(TT - 1):
                    m = pe.matmul(PS[:, 2, c * P:(c + 1) * P], KST[:, c], ITM[:, c], start=True, stop=True)
                u_mm = PE.mark(m)
                step("kst used", u_mm)
            if n == 5:
                wait(dve, latest("state used"))
                st = do(DV, [u_mm], dve.tensor_copy, STATE[:, 0], PS[:, 2, 0:P])
                for c in range(1, TT - 1):
                    st = do(DV, [st, qs_t], dve.scalar_tensor_tensor, out=STATE[:, c], in0=STATE[:, c - 1], scalar=DEC[:, c:c + 1],
                            in1=PS[:, 2, c * P:(c + 1) * P], op0=ALU.mult, op1=ALU.add)
                step("bank 2 read", st)
            if n == 7:
                t_g = sigmoid(SIGG[:, :], XG[:, :], [xg_t])
            if n == 9:
                gs_t = do(DV, [t_g, xg_t], dve.tensor_tensor, GS[:, :], XG[:, :], SIGG[:, :], ALU.mult)
        step("qk used", mm[7])
        run()
        if not last:
            take_qf(marks)
            feed()
        wait(pe, latest("bank 3 read"))
        wait(pe, kept, st, qs_t)
        for c in range(TT):
            cols = slice(c * P, (c + 1) * P)
            m = pe.matmul(PS[:, 3, cols], ITM[:, c], PAIRS[:, c], start=True, stop=c == 0)
            if c:
                m = pe.matmul(PS[:, 3, cols], STATE[:, c - 1], QS[:, cols], start=False, stop=True)
        o_mm = PE.mark(m)
        for name in ("itm", "state", "qs", "pairs"):
            step(name + " used", o_mm)
        wait(act, latest("sqo used"))
        s = do(AC, [o_mm], act.activation, SQO[:, 0], PS[:, 3], ACT.Square)
        o_t = do(DV, [s, gs_t], dve.tensor_tensor, OAR[:, bass.ds(h, 1)].rearrange("p a s -> p (a s)"), PS[:, 3], GS[:, :], ALU.mult)
        step("bank 3 read", o_t)
        step("gs used", o_t)
        wait(dve, latest("ssqo used"))
        ssq = do(DV, [s], dve.tensor_tensor, SSQ[:, :], SSQ[:, :], SQO[:, 0], ALU.add)
        step("sqo used", ssq)
        step("ssqo used", ssq)
        return o_t, ssq

    take_qf(qf_mm)
    wait(pe, latest("bank 0 read"), latest("bank 1 read"))
    wait(act, latest("xc ready"))
    wait(dve, latest("xc ready"))
    with wloop(HG - 1, 2) as i:
        hgrn_head(i, False)
    o_t, ssq = hgrn_head(HG - 1, True)

    def take_qk(marks):
        wait(act, latest("fqk used"))
        t = do(AC, [marks[0]], act.activation, FQ[:, :], PS[:, 4], ACT.Copy)
        step("bank 4 read", t)
        t = do(AC, [marks[1]], act.activation, FK[:, :], PS[:, 5], ACT.Copy)
        step("bank 5 read", t)
        step("fqk ready", t)

    def project_v():
        slot = take()
        mm = linear(6, slot, 0, P, A)
        used(mm)
        feed()
        wait(act, latest("fvf used"))
        t = do(AC, [mm], act.activation, FVF[:, :], PS[:, 6], ACT.Copy)
        step("bank 6 read", t)
        return t

    def turn_v(t):
        wait(pe, latest("bank 5 read"))
        wait(pe, t)
        for c in range(TT):
            m = pe.transpose(PS[:, 5, c * P:(c + 1) * P], FVF[:, c * P:(c + 1) * P], IDENT[:, :])
        t = PE.mark(m)
        step("fvf used", t)
        wait(act, latest("fv used"))
        t = do(AC, [t], act.activation, FV[:, :, :], PS[:, 5].rearrange("p (c t) -> p c t", t=P), ACT.Copy)
        step("bank 5 read", t)
        step("fv ready", t)

    slot = take()
    run, marks = projection((4, 5), slot)
    run()
    take_qk(marks)
    feed()
    turn_v(project_v())
    OAH2, OAL2 = sb("OAH2", [P, DB, S], F32R, R + 64), sb("OAL2", [P, DB, S], F32R, R + 80)
    TO = sb("TO", [P, 2, S], F32, R + 110)
    r = root_mean(7, sum_of_blocks(7, [ssq]), D, RIN[:, :])
    SMF, PTF = sb("SMF", [P, 1, 10 * P], F32, R + 96), sb("PTF", [P, TT, S], F32, R + 101)
    STATF = sb("STATF", [P, 32], F32, R + 109)

    def normed_block(d):
        blk = bass.ds(d, 1)
        hi, lo = OAH2[:, blk], OAL2[:, blk]
        t = do(DV, [r, latest("to used")], dve.tensor_tensor, TO[:, 0:1], OAR[:, blk], RIN[:, :].rearrange("p (a s) -> p a s", a=1), ALU.mult)
        t = do(DV, [t], dve.tensor_scalar, TO[:, 1], TO[:, 0], VEC[:, bass.ds(d + VEC_AT["hg_norm_g_2"], 1)], None, ALU.mult)
        t = do(AC, [t], act.activation, hi, TO[:, 1:2], ACT.Copy)
        t = do(DV, [t], dve.tensor_tensor, lo, TO[:, 1:2], hi.bitcast(F32), ALU.subtract)
        step("to used", t)
        return t

    def fox_head(h, last):
        wait(dve, latest("pickh used"))
        pick_t = do(DV, [], dve.tensor_scalar, PICKH[0:FOX, :], ONES[0:FOX, :], IDENT[0:FOX, bass.ds(h, 1)], None, ALU.mult)
        wait(pe, latest("fqk ready"))
        parts = causal_softmax(SMF, STATF, 0, FQ[:, :], FK[:, :], MASKC, P ** -0.5, (0, 1, 2, 3), [pick_t],
                               key_bias=(PICKH[0:FOX, :], NEGC[0:FOX, :]))
        scored = PE.now()
        step("fqk used", scored)
        step("pickh used", scored)
        if not last:
            slot = take()
            run, marks = projection((4, 5), slot)
            run()
            take_qk(marks)
            feed()
        pt_t = transposed(PTF, parts, (0, 1, 2, 3), 0)
        if not last:
            v_t = project_v()
        normed_block(h)
        wait(pe, latest("bank 7 read"), latest("fv ready"))
        o_mm = weighted_values(PTF, PS[:, 7], [FV[:, j] for j in range(TT)], pt_t, None)
        step("fv used", o_mm)
        blk = bass.ds(h, 1)
        hi, lo = (x[:, blk].rearrange("p a s -> p (a s)") for x in (OBH2, OBL2))
        t = do(AC, [o_mm], act.activation, hi, PS[:, 7], ACT.Copy)
        t = do(DV, [t], dve.tensor_tensor, lo, PS[:, 7], hi.bitcast(F32), ALU.subtract)
        step("bank 7 read", t)
        if not last:
            turn_v(v_t)
        return t, o_mm

    meet()
    with wloop(FOX - 1, 2) as i:
        fox_head(i, False)
    ob_t, o_mm = fox_head(FOX - 1, True)

    ZH2, ZL2 = sb("ZH2", [P, DB, S], F32R, R + 32), sb("ZL2", [P, DB, S], F32R, R + 48)
    SG2, TZ2 = sb("SG2", [P, 2, S], F32, R + 96), sb("TZ2", [P, 2, S], F32, R + 100)
    wait(act, ob_t)
    wait(pe, ob_t)
    wait(dve, ob_t, o_mm)
    OA2 = [(OAH2[:, k], OAL2[:, k]) for k in range(DB)]
    OB2 = [(OBH2[:, k], OBL2[:, k]) for k in range(DB)]
    z_t = gated_sum(DB, A, OA2, OB2, SG2, TZ2, ZH2, ZL2, VEC_AT["b_gate_2"])
    Z = [(ZH2[:, k], ZL2[:, k]) for k in range(DB)]

    MH, ML = sb("MH", [P, DB, MEM], F32R, R), sb("ML", [P, DB, MEM], F32R, R + 8)
    MEMT = sb("MEMT", [P, DB, MEM], F32, R + 16)
    OMH, OML2 = sb("OMH", [P, DB, S], F32R, R + 32), sb("OML2", [P, DB, S], F32R, R + 48)
    MQ, MK, MV = sb("MQ", [P, 2, S], F32, R + 64), sb("MK", [P, 2, MEM], F32, R + 68), sb("MV", [P, 2, MEM], F32, R + 70)
    SMM, PTM = sb("SMM", [P, TT, MEM], F32, R + 72), sb("PTM", [P, 2, S], F32, R + 76)
    SQM2, TM = sb("SQM2", [P, 2, MEM], F32, R + 80), sb("TM", [P, 2, MEM], F32, R + 82)
    STATM, RINM = sb("STATM", [P, 16], F32, R + 84), sb("RINM", [P, MEM], F32, R + 85)
    s_mem = g.track("memory")
    wait(act, z_t.last())
    mem_t = s_mem.mark(act.dma_start(MEMT[:, :, :], io["memT"].rearrange("(k p) n -> p k n", p=P)), by=16)

    def norm_memory():
        wait(pe, latest("bank 7 read"))
        for d in range(DB):
            wait(act, latest(f"sqm2_{d % 2} used"))
            t = do(AC, [mem_t], act.activation, SQM2[:, d % 2], MEMT[:, d], ACT.Square)
            mm = do(PE, [t], pe.matmul, PS[:, 7, 0:MEM], ONES[:, :], SQM2[:, d % 2], start=d == 0, stop=d == DB - 1)
            step(f"sqm2_{d % 2} used", mm)
        r = root_mean(7, mm, D, RINM[:, :])
        for d in range(DB):
            wait(dve, latest(f"tm{d % 2} used"))
            t = do(DV, [r], dve.scalar_tensor_tensor, out=TM[:, d % 2], in0=MEMT[:, d], scalar=vec("mem_kv_g_2", d, 1),
                   in1=RINM[:, :], op0=ALU.mult, op1=ALU.mult)
            t = split_from(TM[:, d % 2], MH[:, d], ML[:, d], [t])
            step(f"tm{d % 2} used", t)
        step("memory normed", t)

    Y, y_t = square_linear(Z, [z_t.last()], 88, 98, between=norm_memory)
    x_t = residual(Y, y_t, 0, vec("mix_post_g_2"))
    a_t = prenorm(x_t, vec("mem_pre_g_2"))
    MM = [(MH[:, k], ML[:, k]) for k in range(DB)]

    def mem_q():
        slot = take()
        mm = two_blocks((0, 1), slot, A, a_t)
        used(mm[1])
        wait(act, latest("mq used"))
        for f in range(2):
            q_t = do(AC, [mm[f]], act.activation, MQ[:, f], PS[:, f], ACT.Copy)
            step(f"bank {f} read", q_t)
        feed()
        return q_t

    def mem_k():
        slot = take()
        mm = [linear(2 + f, slot, f * P, 2 * P, MM) for f in range(2)]
        used(mm[1])
        wait(act, latest("mk used"))
        for f in range(2):
            k_t = do(AC, [mm[f]], act.activation, MK[:, f], PS[:, 2 + f, 0:MEM], ACT.Copy)
            step(f"bank {2 + f} read", k_t)
        feed()
        return k_t

    def mem_scores(q_t, k_t):
        wait(pe, latest("bank 4 read"), latest("bank 5 read"))
        wait(pe, q_t, k_t)
        for i in range(TT):
            for f in range(2):
                m = pe.matmul(PS[:, 4 + i // 2, (i % 2) * MEM:(i % 2 + 1) * MEM], MQ[:, f, i * P:(i + 1) * P],
                              MK[:, f], start=f == 0, stop=f == 1)
        mm = PE.mark(m)
        step("mq used", mm)
        step("mk used", mm)
        scale = MEM ** -0.5
        banks = PS[:, 4:6].rearrange("p b (i k) -> p (b i) k", k=MEM)
        high, low, sums, inv = (STATM[:, 4 * n:4 * n + 4] for n in range(4))
        wait(dve, latest("smm used"))
        t = do(DV, [mm], dve.tensor_reduce, high, banks, mybir.AxisListType.X, ALU.max)
        t = do(DV, [t], dve.tensor_scalar, low, high, -scale, None, ALU.mult)
        wait(act, latest("smm used"))
        for i in range(TT):
            e = do(AC, [t], act.activation, SMM[:, i], banks[:, i], ACT.Exp, bias=low[:, i:i + 1], scale=scale,
                   accum_out=sums[:, i:i + 1])
        step("bank 4 read", e)
        step("bank 5 read", e)
        t = do(DV, [e], dve.reciprocal, inv, sums)
        for i in range(TT):
            p_t = do(DV, [t], dve.tensor_scalar, SMM[:, i], SMM[:, i], inv[:, i:i + 1], None, ALU.mult)
        return p_t

    def mem_v():
        slot = take()
        for j in range(2):
            wait(pe, latest(f"bank {6 + j} read"))
            n = 0
            for k in range(DB):
                for wt, x in ((WHI, MH), (WHI, ML), (WLO, MH)):
                    m = pe.matmul(PS[:, 6 + j, 0:MEM], x[:, k, j * P:(j + 1) * P], wt[:, slot, k * MEM:(k + 1) * MEM],
                                  start=n == 0, stop=n == 3 * DB - 1)
                    n += 1
            mm = PE.mark(m)
            wait(act, latest("mv used"))
            v_t = do(AC, [mm], act.activation, MV[:, j], PS[:, 6 + j, 0:MEM], ACT.Copy)
            step(f"bank {6 + j} read", v_t)
        used(mm)
        feed()
        return v_t

    def mem_values(block, p_t, v_t):
        for j in range(2):
            wait(pe, latest(f"bank {4 + j} read"))
        wait(pe, p_t)
        wait(act, latest("ptm used"))
        for j in range(2):
            for i in range(TT):
                m = pe.transpose(PS[:, 4 + j, i * P:(i + 1) * P], SMM[:, i, j * P:(j + 1) * P], IDENT[:, :])
            m = PE.mark(m)
            pt_t = do(AC, [m], act.activation, PTM[:, j], PS[:, 4 + j], ACT.Copy)
            step(f"bank {4 + j} read", pt_t)
        step("smm used", m)
        wait(pe, pt_t, v_t)
        for f in range(2):
            wait(pe, latest(f"bank {6 + f} read"))
            for j in range(2):
                m = pe.matmul(PS[:, 6 + f], MV[:, j, f * P:(f + 1) * P], PTM[:, j], start=j == 0, stop=j == 1)
            m = PE.mark(m)
            hi, lo = (x[:, bass.ds(block + f, 1)].rearrange("p a s -> p (a s)") for x in (OMH, OML2))
            t = do(AC, [m], act.activation, hi, PS[:, 6 + f], ACT.Copy)
            t = do(DV, [t], dve.tensor_tensor, lo, PS[:, 6 + f], hi.bitcast(F32), ALU.subtract)
            step(f"bank {6 + f} read", t)
        step("ptm used", m)
        step("mv used", m)
        return t

    wait(pe, latest("memory normed"), a_t[0])
    wait(act, a_t[-1])
    wait(dve, a_t[-1])
    tables("exp")
    with wloop(MEM_H // 2, 6) as i:
        q_t, k_t = mem_q(), mem_k()
        p_t = mem_scores(q_t, k_t)
        v_t = mem_v()
        q_t = mem_q()
        mem_values(i * 4, p_t, v_t)
        k_t = mem_k()
        p_t = mem_scores(q_t, k_t)
        v_t = mem_v()
        om_t = mem_values(i * 4 + 2, p_t, v_t)
    OM = [(OMH[:, k], OML2[:, k]) for k in range(DB)]
    Y, y_t = square_linear(OM, [om_t.last()], 88, 98)
    x_t = residual(Y, y_t, 0, vec("mem_post_g_2"))
    a_t = prenorm(x_t, vec("ffn2_pre_g_2"))
    x_t = ffn(a_t, coef(7))

    while stream["fed"] < n_chunks:
        feed()

    s_out = nc.alloc_semaphore("s_out")
    for d in range(DB):
        wait(act, x_t[d])
        act.dma_start(io["out"][d * P:(d + 1) * P, :], X[:, d]).then_inc(s_out, 16)
    act.wait_ge(s_out, DB * 16)
    n_taken.append((stream["taken"], stream["fed"]))
    return g.counted


n_taken = []


def weight_chunks(w):
    out = []

    def blocks(a, rows=P):
        return a.reshape(-1, P, a.shape[1]).transpose(1, 0, 2).reshape(P, -1)

    def chunk(*parts):
        a = np.concatenate(parts, 1)
        out.append(np.pad(a, ((0, 0), (0, CH - a.shape[1]))))

    def ffn(gate, up, down):
        for i in range(FB // 2):
            chunk(blocks(gate[:, i * 256:(i + 1) * 256]))
            chunk(blocks(up[:, i * 256:(i + 1) * 256]))
        for c in range(FB // 2):
            chunk(blocks(down[c * 256:(c + 1) * 256]))

    def square(a):
        for i in range(a.shape[1] // 256):
            chunk(blocks(a[:, i * 256:(i + 1) * 256]))

    w1 = {k: v[0] for k, v in w.items()}
    ffn(w1["w_gate1"], w1["w_up1"], w1["w_down1"])
    w_in = np.concatenate([w1["w_in"][:, :712], np.zeros((D, 56), np.float32)], 1)
    for i in range(3):
        chunk(blocks(w_in[:, i * 256:(i + 1) * 256]))
    square(w1["w_in"][:, 2248:2504])
    chunk(blocks(w1["w_iq"].reshape(Q_LORA, -1)))
    square(w1["w_in"][:, 712:2248])
    square(w1["w_in"][:, 2504:3016])
    for i in range(4):
        hs = slice(2 * i, 2 * i + 2)
        chunk(blocks(w1["w_uq"][:, hs].reshape(Q_LORA, -1)), blocks(w1["w_uk"][:, hs].reshape(KV_LORA, -1)),
              blocks(w1["w_uv"][:, hs].reshape(KV_LORA, -1)))
    for d in range(DB):
        c = slice(d * P, (d + 1) * P)
        chunk(blocks(w1["w_in"][:, 3016:4040][:, c]), blocks(w1["w_up_b"][:, c]))
        chunk(blocks(w1["w_in"][:, 4040:5064][:, c]), blocks(w1["w_up_a"][:, c]))
    square(w1["w_o"])
    ffn(w1["w_gate2"], w1["w_up2"], w1["w_down2"])
    w2 = {k[:-2]: v[0] for k, v in w.items() if k.endswith("_2") and v.ndim == 3}
    ffn(w2["ffn1_w_in"][:, :FF], w2["ffn1_w_in"][:, FF:], w2["ffn1_w_down"])
    q_a, f_a, i_a, g_a, q_b, k_b, v_b = (w2["w_in"][:, n * D:(n + 1) * D] for n in range(7))
    f_b, gates = w2["w_in"][:, 7 * D:7 * D + FOX], w2["w_in"][:, 7 * D + FOX:]

    def pair(a, b, h):
        c = slice(h * P, (h + 1) * P)
        chunk(blocks(np.concatenate([a[:, c], b[:, c]], 1)))

    pair(q_a, f_a, 0)
    chunk(blocks(np.pad(f_b, ((0, 0), (0, P - FOX)))))
    for h in range(HG):
        pair(i_a, g_a, h)
        if h < HG - 1:
            pair(q_a, f_a, h + 1)
    pair(q_b, k_b, 0)
    for h in range(FOX):
        chunk(blocks(v_b[:, h * P:(h + 1) * P]))
        if h < FOX - 1:
            pair(q_b, k_b, h + 1)
    for d in range(DB):
        c = slice(d * P, (d + 1) * P)
        chunk(blocks(gates[:, :D][:, c]), blocks(w2["w_branch_b"][:, c]))
        chunk(blocks(gates[:, D:][:, c]), blocks(w2["w_branch_a"][:, c]))
    square(w2["w_out"])
    for h in range(MEM_H):
        c = slice(h * MEM, (h + 1) * MEM)
        for a in (w2["w_mq"], w2["w_mkv"][:, :D], w2["w_mkv"][:, D:]):
            chunk(blocks(a[:, c]))
    square(w2["w_mo"])
    ffn(w2["ffn2_w_in"][:, :FF], w2["ffn2_w_in"][:, FF:], w2["ffn2_w_down"])
    if len(out) % 2:
        out.append(out[-1])
    return np.stack(out)


_STAGE = "end"


def kernel(**inputs):
    import concourse.bacc as _bacc
    from concourse.bass_utils import run_bass_kernel_spmd as _run

    w = {k: np.asarray(v) for k, v in inputs.items()}
    mod_w = w["w_mod"][0].reshape(DB, P, NMOD, P).transpose(1, 2, 0, 3).reshape(P, NMOD, D)
    arrays = {
        "xT": np.ascontiguousarray(w["x"][0].T),
        "memT": np.ascontiguousarray(w["mem_2"][0].T),
        "positions": np.ascontiguousarray(w["positions"]),
        "fox_bias": np.ascontiguousarray(w["fox_f_bias_2"].reshape(FOX, 1)),
        "vecs": np.ascontiguousarray(np.concatenate([w[n].reshape(-1, P) for n, _ in VECS]).T),
        "w_mod": np.ascontiguousarray(np.pad(mod_w, ((0, 0), (0, MBLK), (0, 0)))),
        "weights": weight_chunks(w),
        "consts": CONSTS,
    }
    counts = {}
    for _ in range(2):
        nc = _bacc.Bacc("TRN2", target_bir_lowering=False, num_devices=1, dynamic_dma_scratch_size=256)
        io = {n: nc.dram_tensor(f"in_{n}", a.shape, mybir.dt.from_np(a.dtype), kind="ExternalInput").ap()
              for n, a in arrays.items()}
        io["out"] = nc.dram_tensor("out_xT", (D, S), F32, kind="ExternalOutput").ap()
        counts = build(nc, io, counts, _STAGE)
    r = _run(nc, [{f"in_{n}": a for n, a in arrays.items()}], core_ids=[0])
    return np.ascontiguousarray(r.results[0]["out_xT"].T)[None]
```
